# Optimizing a Trainium2 kernel written in Bass

```python
import math
import jax, jax.numpy as jnp
from jax import lax
import numpy as np

D_MODEL = 2048
BATCH = 1
SEQ = 256
DEPTH = 2
DEC_BATCH = 8
DEC_SEQ = 8
PAST_LEN = 2048
PAGE_SIZE = 128

N_EVEN = (DEPTH + 1) // 2
N_ODD = DEPTH // 2
ATTN_HEADS = 16
KV_HEADS = 4
HEAD_DIM = 64
GQA_GROUP = ATTN_HEADS // KV_HEADS
ATTN_WIDTH = ATTN_HEADS * HEAD_DIM
KV_WIDTH = KV_HEADS * HEAD_DIM
WINDOW = 128
HGRN_DK = 128
HGRN_DV = 128
HGRN_HEADS = (D_MODEL // 2) // HGRN_DK
HGRN_WIDTH = HGRN_HEADS * HGRN_DK
HGRN_VWIDTH = HGRN_HEADS * HGRN_DV
HGRN_CHUNK = 64
CONV_WIDTH = D_MODEL
CONV_K = 3
EVEN_IN = 2 * ATTN_WIDTH + 2 * KV_WIDTH + 2 * HGRN_WIDTH + 2 * HGRN_VWIDTH
EVEN_MIX = ATTN_WIDTH + HGRN_VWIDTH
ODD_IN = 4 * CONV_WIDTH
RMS_EPS = 1e-6
MASK_VALUE = -1e30
MIN_FORGET = 1e-20

kernel_name = 'hybrid_swa_hgrn2_shortconv_step'

def rms_norm(x, w):
    xf = x.astype(jnp.float32)
    y = xf * lax.rsqrt(jnp.mean(xf * xf, axis=-1, keepdims=True) + RMS_EPS)
    return (y * w.astype(jnp.float32)).astype(x.dtype)

def split_cols(a, sizes):
    idx = np.cumsum(sizes)[:-1].tolist()
    return jnp.split(a, idx, axis=-1)

def swa_sinks(q, k, v, k_past, v_past, sinks, past_valid):
    B, L = q.shape[0], q.shape[1]
    qb_len = WINDOW if L % WINDOW == 0 else L
    nb = L // qb_len
    span = WINDOW + qb_len
    k_ext = jnp.concatenate([k_past.astype(k.dtype), k], axis=1)
    v_ext = jnp.concatenate([v_past.astype(v.dtype), v], axis=1)
    idx = (jnp.arange(nb) * qb_len)[:, None] + jnp.arange(span)[None, :]
    kb = k_ext[:, idx]
    vb = v_ext[:, idx]
    qb = q.reshape(B, nb, qb_len, KV_HEADS, GQA_GROUP, HEAD_DIM)
    s = jnp.einsum('bnqkgd,bnskd->bnkgqs', qb, kb).astype(jnp.float32) * (HEAD_DIM ** -0.5)
    j = jnp.arange(qb_len)[:, None]
    r = jnp.arange(span)[None, :]
    in_band = (r >= j) & (r <= j + WINDOW)
    has_key = (idx >= WINDOW) | past_valid
    mask = in_band[None] & has_key[:, None, :]
    s = jnp.where(mask[None, :, None, None], s, MASK_VALUE)
    sink = jnp.broadcast_to(
        sinks.astype(jnp.float32).reshape(KV_HEADS, GQA_GROUP)[None, None, :, :, None, None],
        s.shape[:-1] + (1,))
    p = jax.nn.softmax(jnp.concatenate([s, sink], axis=-1), axis=-1)[..., :-1]
    o = jnp.einsum('bnkgqs,bnskd->bnqkgd', p.astype(v.dtype), vb)
    return o.reshape(B, L, ATTN_WIDTH), k_ext[:, -WINDOW:], v_ext[:, -WINDOW:]

def hgrn2_recurrence(q, k, v, log_f, s0):
    B, L, H, DK = q.shape
    DV = v.shape[-1]
    c = HGRN_CHUNK if L % HGRN_CHUNK == 0 else L
    n = L // c

    def chunks(a):
        return a.astype(jnp.float32).reshape(B, n, c, H, a.shape[-1]).transpose(1, 0, 3, 2, 4)

    causal = jnp.tril(jnp.ones((c, c), dtype=bool))[:, :, None]

    def step(S, inp):
        qc, kc, vc, gc = inp
        b = jnp.cumsum(gc, axis=2)
        diff = b[:, :, :, None, :] - b[:, :, None, :, :]
        decay = jnp.where(causal, jnp.exp(jnp.where(causal, diff, 0.0)), 0.0)
        scores = jnp.einsum('bhtd,bhsd,bhtsd->bhts', qc, kc, decay)
        o = (jnp.einsum('bhts,bhse->bhte', scores, vc)
             + jnp.einsum('bhtd,bhde->bhte', qc * jnp.exp(b), S))
        b_end = b[:, :, -1:, :]
        S_new = (jnp.exp(b_end[:, :, 0, :])[..., None] * S
                 + jnp.einsum('bhsd,bhse->bhde', kc * jnp.exp(b_end - b), vc))
        return S_new, o

    s_final, o = lax.scan(step, s0.astype(jnp.float32),
                          (chunks(q), chunks(k), chunks(v), chunks(log_f)))
    o = o.transpose(1, 0, 3, 2, 4).reshape(B, L, H, DV)
    return o, s_final

def even_mixer(h, k_past, v_past, s0, past_valid, w_in, w_out, qn, kn, sinks, lb, hn):
    B, L, _ = h.shape
    proj = h @ w_in
    q_a, k_a, v_a, z_a, q_b, f_b, i_b, z_b = split_cols(
        proj, (ATTN_WIDTH, KV_WIDTH, KV_WIDTH, ATTN_WIDTH,
               HGRN_WIDTH, HGRN_WIDTH, HGRN_VWIDTH, HGRN_VWIDTH))
    q_a = rms_norm(q_a.reshape(B, L, ATTN_HEADS, HEAD_DIM), qn)
    k_a = rms_norm(k_a.reshape(B, L, KV_HEADS, HEAD_DIM), kn)
    v_a = v_a.reshape(B, L, KV_HEADS, HEAD_DIM)
    o_a, k_buf, v_buf = swa_sinks(q_a, k_a, v_a, k_past, v_past, sinks, past_valid)
    a = f_b.astype(jnp.float32)
    lb = lb.astype(jnp.float32)
    f = lb + (1.0 - lb) * jax.nn.sigmoid(a)
    log_f = jnp.log(jnp.maximum(f, MIN_FORGET))
    k_b = (1.0 - lb) * jax.nn.sigmoid(-a)
    q_b = q_b.astype(jnp.float32) * (HGRN_DK ** -0.5)
    o_b, s_new = hgrn2_recurrence(
        q_b.reshape(B, L, HGRN_HEADS, HGRN_DK), k_b.reshape(B, L, HGRN_HEADS, HGRN_DK),
        i_b.reshape(B, L, HGRN_HEADS, HGRN_DV), log_f.reshape(B, L, HGRN_HEADS, HGRN_DK), s0)
    o_b = rms_norm(o_b, hn).reshape(B, L, HGRN_VWIDTH).astype(h.dtype)
    mix = jnp.concatenate([o_a * jax.nn.silu(z_a), o_b * jax.nn.silu(z_b)], axis=-1)
    return mix @ w_out, k_buf, v_buf, s_new

def odd_mixer(h, buf, w_in, conv_w, w_out):
    L = h.shape[1]
    u, g_in, g_out, z = split_cols(h @ w_in, (CONV_WIDTH, CONV_WIDTH, CONV_WIDTH, CONV_WIDTH))
    cin = g_in * u
    ext = jnp.concatenate([buf.astype(cin.dtype), cin], axis=1)
    conv = ext[:, 0:L] * conv_w[0]
    for i in range(1, CONV_K):
        conv = conv + ext[:, i:i + L] * conv_w[i]
    y = g_out * conv * jax.nn.silu(z)
    return y @ w_out, ext[:, -(CONV_K - 1):]

def run_trunk(x, c, cache_k, cache_v, state_hgrn, state_conv, past_valid,
              norm_w, ada_w, ada_b, even_w_in, even_w_out, q_norm_w, k_norm_w, attn_sinks,
              hgrn_lb_logits, hgrn_norm_w, odd_w_in, odd_conv_w, odd_w_out):
    sm = jax.nn.softmax(hgrn_lb_logits.astype(jnp.float32), axis=0)
    lower_bounds = jnp.cumsum(sm, axis=0) - sm[0:1]
    cond = jax.nn.silu(c.astype(jnp.float32))
    ks, vs, ss, cs = [], [], [], []
    for layer in range(DEPTH):
        mod = (cond @ ada_w[layer].astype(jnp.float32)
               + ada_b[layer].astype(jnp.float32)).astype(x.dtype)[:, None, :]
        shift, scale, gate = jnp.split(mod, 3, axis=-1)
        h = rms_norm(x, norm_w[layer]) * (1 + scale) + shift
        if layer % 2 == 0:
            e = layer // 2
            out, kb, vb, sn = even_mixer(h, cache_k[e], cache_v[e], state_hgrn[e], past_valid,
                                         even_w_in[e], even_w_out[e], q_norm_w[e], k_norm_w[e],
                                         attn_sinks[e], lower_bounds[e], hgrn_norm_w[e])
            ks.append(kb)
            vs.append(vb)
            ss.append(sn)
        else:
            o = layer // 2
            out, cb = odd_mixer(h, state_conv[o], odd_w_in[o], odd_conv_w[o], odd_w_out[o])
            cs.append(cb)
        x = x + gate * out
    return x, jnp.stack(ks), jnp.stack(vs), jnp.stack(ss), jnp.stack(cs)

def setup_inputs(seed: int = 0) -> dict:
    key = jax.random.key(seed)
    k = jax.random.split(key, 21)
    f32 = jnp.float32

    def nrm(kk, shape, scale):
        return jax.random.normal(kk, shape, f32) * scale

    return {
        'x_prompt': nrm(k[0], (BATCH, SEQ, D_MODEL), 1.0),
        'x_sample': nrm(k[1], (DEC_BATCH, DEC_SEQ, D_MODEL), 1.0),
        'cache_k': nrm(k[2], (N_EVEN, DEC_BATCH, WINDOW, KV_HEADS, HEAD_DIM), 1.0),
        'cache_v': nrm(k[3], (N_EVEN, DEC_BATCH, WINDOW, KV_HEADS, HEAD_DIM), 1.0),
        'state_hgrn': nrm(k[4], (N_EVEN, DEC_BATCH, HGRN_HEADS, HGRN_DK, HGRN_DV), 0.5),
        'state_conv': nrm(k[5], (N_ODD, DEC_BATCH, CONV_K - 1, CONV_WIDTH), 1.0),
        'c_prompt': nrm(k[6], (BATCH, D_MODEL), 1.0),
        'c_sample': nrm(k[7], (DEC_BATCH, D_MODEL), 1.0),
        'norm_w': 1.0 + nrm(k[8], (DEPTH, D_MODEL), 0.02),
        'ada_w': nrm(k[9], (DEPTH, D_MODEL, 3 * D_MODEL), 0.5 * D_MODEL ** -0.5),
        'ada_b': nrm(k[10], (DEPTH, 3 * D_MODEL), 0.02),
        'even_w_in': nrm(k[11], (N_EVEN, D_MODEL, EVEN_IN), D_MODEL ** -0.5),
        'even_w_out': nrm(k[12], (N_EVEN, EVEN_MIX, D_MODEL), EVEN_MIX ** -0.5),
        'q_norm_w': 1.0 + nrm(k[13], (N_EVEN, HEAD_DIM), 0.02),
        'k_norm_w': 1.0 + nrm(k[14], (N_EVEN, HEAD_DIM), 0.02),
        'attn_sinks': nrm(k[15], (N_EVEN, ATTN_HEADS), 0.5),
        'hgrn_lb_logits': nrm(k[16], (N_EVEN, HGRN_WIDTH), 0.5),
        'hgrn_norm_w': 1.0 + nrm(k[17], (N_EVEN, HGRN_DV), 0.02),
        'odd_w_in': nrm(k[18], (N_ODD, D_MODEL, ODD_IN), D_MODEL ** -0.5),
        'odd_conv_w': nrm(k[19], (N_ODD, CONV_K, CONV_WIDTH), CONV_K ** -0.5),
        'odd_w_out': nrm(k[20], (N_ODD, CONV_WIDTH, D_MODEL), CONV_WIDTH ** -0.5),
    }

def reference(x_prompt, x_sample, cache_k, cache_v, state_hgrn, state_conv, c_prompt, c_sample,
              norm_w, ada_w, ada_b, even_w_in, even_w_out, q_norm_w, k_norm_w, attn_sinks,
              hgrn_lb_logits, hgrn_norm_w, odd_w_in, odd_conv_w, odd_w_out):
    b_p = x_prompt.shape[0]
    dt = x_prompt.dtype
    zk = jnp.zeros((N_EVEN, b_p, WINDOW, KV_HEADS, HEAD_DIM), dt)
    zs = jnp.zeros((N_EVEN, b_p, HGRN_HEADS, HGRN_DK, HGRN_DV), jnp.float32)
    zc = jnp.zeros((N_ODD, b_p, CONV_K - 1, CONV_WIDTH), dt)
    y_prompt, ck_p, cv_p, sh_p, sc_p = run_trunk(
        x_prompt, c_prompt, zk, zk, zs, zc, False,
        norm_w, ada_w, ada_b, even_w_in, even_w_out, q_norm_w, k_norm_w, attn_sinks,
        hgrn_lb_logits, hgrn_norm_w, odd_w_in, odd_conv_w, odd_w_out)
    y_sample, ck_s, cv_s, sh_s, sc_s = run_trunk(
        x_sample, c_sample, cache_k, cache_v, state_hgrn, state_conv, True,
        norm_w, ada_w, ada_b, even_w_in, even_w_out, q_norm_w, k_norm_w, attn_sinks,
        hgrn_lb_logits, hgrn_norm_w, odd_w_in, odd_conv_w, odd_w_out)
    return (y_prompt, y_sample, ck_p, cv_p, sh_p, sc_p, ck_s, cv_s, sh_s, sc_s)


_drawn_inputs = setup_inputs


def setup_inputs(seed=0):
    import zlib

    import numpy as np

    out = dict(_drawn_inputs(seed))
    spreads = {}
    factors = {'q_norm_w': 42.924, 'k_norm_w': 8.572, 'attn_sinks': 64.0, 'hgrn_norm_w': 24.144}
    for name, (base, spread) in spreads.items():
        noise = np.random.default_rng([zlib.crc32(name.encode()), seed]).standard_normal(out[name].shape)
        drawn = base * np.exp(spread * noise) if base else spread * noise
        out[name] = __import__('jax').numpy.asarray(drawn.astype(out[name].dtype))
    for name, factor in factors.items():
        out[name] = (out[name] * factor).astype(out[name].dtype)
    return out
```

```python
from contextlib import ExitStack

import concourse.bass as bass
from concourse import mybir

F32 = mybir.dt.float32
F32R = mybir.dt.float32r
ALU = mybir.AluOpType
ACT = mybir.ActivationFunctionType
AX = mybir.AxisListType
ds = bass.ds

P = 128
D = 2048
KC = D // P
SEQ, NB, NJ = 256, 8, 8
NS = NB * NJ
T = SEQ + NS
NSEQ = 1 + NB
UC = 256
QK = 4
HEADS, KVH, HD, WIN = 16, 4, 64, 128
HH, DK = 8, 128
EPS = 1e-6
LN16 = 2.772588722239781
LEVELS = [32, 16, 8, 4, 2, 1]
NL = len(LEVELS)

U_KV, U_Q, U_QB, U_F, U_I, U_ZA, U_ZB, U_OUT0, U_IN1, U_OUT1 = 0, 2, 6, 10, 14, 18, 22, 26, 34, 66
U_END = 74
C_Q, C_K, C_V, C_QB, C_S, C_KB, C_I, C_Z = 0, 8, 10, 12, 20, 28, 36, 44
C_END = 60
C_X0 = C_Z
C_X1 = 0
C_Y = 20
C_IN = 0
GA = 16


class Steps:

    def __init__(self, eng, sem):
        self.eng, self.sem, self.n, self.reg, self.per = eng, sem, 0, None, 0

    def __call__(self, ins):
        ins.then_inc(self.sem, 1)
        self.n += 1
        return ins

    def settle(self):
        self.eng.wait_ge(self.sem, self.n if self.reg is None else self.reg * self.per + self.n)

    def enter(self, reg, per):
        self.reg, self.per, self.start = reg, per, self.n

    def leave(self, times):
        assert self.n - self.start == self.per, (self.n - self.start, self.per)
        self.n = self.start + self.per * times
        self.reg = None


def hybrid_step_kernel(nc, a, o):
    ctx = ExitStack()

    def sem(name):
        return ctx.enter_context(nc.semaphore(name))

    at = [16512]

    def sb(name, shape, dt=F32, where=None):
        size = 4
        for n in shape[1:]:
            size *= n
        size = (size + 31) // 32 * 32
        if where is None:
            where = at[0]
            at[0] += size
        return nc.alloc_sbuf_tensor_at(name, shape, dt, offset=where)

    raw = sb("raw", [P, 4, QK, UC])
    wh = sb("wh", [P, 4, QK, UC], F32R)
    o_wl = at[0]
    wl = sb("wl", [P, 4, QK, UC], F32R)
    adaw2 = sb("adaw2", [P, 4, QK, UC], F32, o_wl)
    adaw = sb("adaw", [P, 4, QK, UC])
    o_h = at[0]
    hh = sb("hh", [P, KC, T], F32R)
    hl = sb("hl", [P, KC, T], F32R)
    o_acts = at[0]
    acts = sb("acts", [P, C_END, T])
    yh = sb("yh", [P, KC, T], F32R, o_acts + C_Y * T * 4)
    yl = sb("yl", [P, KC, T], F32R, o_acts + (C_Y + KC) * T * 4)
    ident = sb("ident", [P, P])
    ones = sb("ones", [P, P])
    blk = sb("blk", [P, P])
    sel = sb("sel", [P, NSEQ])
    seqm = sb("seqm", [NS, NB])
    rmask = sb("rmask", [P, T])
    lmask = sb("lmask", [P, NL + 1, 64])
    pmask = sb("pmask", [P, 384])
    smask = sb("smask", [P, WIN + NB * NS])
    rep8 = sb("rep8", [NJ, P])
    cond = sb("cond", [P, KC, 32])
    mods = sb("mods", [P, 96, NSEQ])
    vecs = sb("vecs", [P, 96 + 92])
    s1 = sb("s1", [P, KC, NSEQ])
    adas = sb("adas", [P, UC])
    sct = sb("sct", [P, KC, 2 * NB])
    sinkp = sb("sinkp", [P, HEADS])
    sinks = sb("sinks", [P, 1])
    small = sb("small", [P, 32])
    lb = sb("lb", [P, 4, HH])
    stmp = sb("stmp", [P, 2 * NS])
    norm = sb("norm", [P, 1280])
    soft = sb("soft", [P, 1280])
    assert at[0] <= nc.sbuf_usable_end, at[0]
    print("sbuf left", nc.sbuf_usable_end - at[0])

    ssq, rstd, hb = norm[:, 0:T], norm[:, T:2 * T], norm[:, 2 * T:4 * T].rearrange("p (a t) -> p a t", a=2)
    hbs = [hb, soft[:, 2 * T:4 * T].rearrange("p (a t) -> p a t", a=2)]
    adab = vecs[:, 0:96]
    V2 = 96
    nw = vecs[:, V2:V2 + 32]
    cw = vecs[:, V2 + 32:V2 + 80].rearrange("p (i c) -> p i c", i=3)
    lbl = vecs[:, V2 + 80:V2 + 88]
    qn, kn, hn = (vecs[:, V2 + 88 + n:V2 + 89 + n] for n in range(3))

    def cols(c0, n, w, rows=P):
        return acts[0:rows, c0:c0 + (n * w + T - 1) // T, :].rearrange("p c t -> p (c t)")[:, 0:n * w].rearrange(
            "p (n w) -> p n w", n=n)

    xnat = cols(0, 3, D)
    cnat = cols(20, 1, D, NSEQ)
    scnat = cols(28, 1, D, 2 * NB)
    vnat1 = cols(36, 1, P, 96)
    vnat2 = cols(37, 1, P, 91)
    m8 = cols(38, 1, WIN + NB * 72, NJ)
    xsq = cols(41, 2, T)

    def scratch(name, shape, off):
        return sb(name, shape, F32, o_h + 4 * off)

    p4 = scratch("p4", [P, 4, 384], 0)
    qs2 = scratch("qs2", [P, 2, NB, 4, NJ], 2048)
    knat = scratch("knat", [P, 3, 256], 2560)
    vnat = scratch("vnat", [P, 3, 256], 3328)
    vc = scratch("vc", [P, NB, 256], 4096)
    kct = scratch("kct", [P, NB, 2, P], 6144)
    ckn = scratch("ckn", [P, NB, 256], 8192)
    pt2 = soft[:, 0:1024].rearrange("p (a k) -> p a k", a=2)
    ksw = norm[:, 0:2 * T].rearrange("p (c t) -> p c t", c=2)
    HB = NL * SEQ + 3 * NS + 2 * T
    hbufs = [scratch("hbuf0", [P, HB], 0), sb("hbuf1", [P, HB], F32, o_acts)]
    qebs = [scratch("qeb0", [P, T], HB), sb("qeb1", [P, T], F32, o_acts + 4 * HB)]
    vn = scratch("vn", [P, 3, P], 2688)
    ken = scratch("ken", [P, 3, P], 3072)
    sctmp = scratch("sctmp", [P, 3, 448], 3456)
    stt_ = scratch("stt", [P, 3, 64], 4800)
    sst = scratch("sst", [P, 4, P], 4992)
    s0 = scratch("s0", [P, 2, NB, P], 5504)
    vz = scratch("vz", [NS, NB, P], 7552)
    osb = scratch("osb", [P, T], 8576)
    osq = scratch("osq", [P, T], 8896)
    fg = scratch("fg", [P, T], 9216)
    om = scratch("om", [P, 2, T], 9536)

    xspill = nc.dram_tensor("xspill", [P, KC * T], F32, kind="Internal").ap()

    bank = [ctx.enter_context(nc.psum_tensor(f"bank{n}", [P, 512], F32)) for n in range(4)]
    pproj = ctx.enter_context(nc.psum_tensor("pproj", [P, 4, 512], F32))

    s_wq = [sem(f"w_landed{n}") for n in range(4)]
    s_aq = [sem(f"ada_landed{n}") for n in range(4)]
    s_aq2 = [sem(f"ada2_landed{n}") for n in range(4)]
    h_nrm, h_aff = sem("h_normed"), sem("h_affine")
    s_cst, s_vec, s_xin, s_cin, s_scin = (sem(x) for x in ("const_landed", "vec_landed", "x_landed", "c_landed", "sc_landed"))
    hi_ready, lo_ready, quarter_used = (sem(x) for x in ("hi_ready", "lo_ready", "quarter_used"))
    h_sq, xc_new, lb_exp = sem("squared"), sem("x1_written"), sem("lb_exp")
    hp_out = sem("prompt_state_stored")
    bank_free = [sem("bank_free0"), sem("bank_free1")]
    h_hi, h_ready, hb_ready = sem("h_hi"), sem("h_ready"), sem("hb_ready")
    ada_used, ada_out, ada_sel, mod_done = (sem(x) for x in ("ada_used", "ada_out", "ada_sel", "mod_done"))
    pool_s, dve_s, act_s = sem("pool_steps"), sem("dve_steps"), sem("act_steps")
    consts = sem("consts")
    s_tp, s_tpe = sem("start_transposed"), sem("start_evacuated")
    vecs_done = sem("vecs_done")
    csig, cond_done = sem("csig"), sem("cond_done")
    stored, x1_loaded = sem("x_and_conv_state_stored"), sem("x_reloaded")
    ss_done, ss_sum, ms_ready, rs_ready = sem("ss_done"), sem("ss_summed"), sem("ms_ready"), sem("rs_ready")
    sqr = sem("sq_ready")
    xc_act = sem("xt_written")
    z_sig = sem("z_sigmoid")
    cache_in, kv_out = sem("caches_landed"), sem("kv_stored")
    n_sq, n_sum, n_ms, n_y, n_q = (sem(x) for x in ("qk_squared", "qk_summed", "qk_mean", "qk_rsqrt", "qk_normed"))
    t_ps, t_sb, k_sw, j_rs = sem("kv_transposed"), sem("kv_evacuated"), sem("k_exchanged"), sem("job_scale")
    q_st, c_ps, c_sb = sem("sample_queries"), sem("cached_k_transposed"), sem("cached_k_ready")
    j_sc, j_max, j_exp, j_p, j_pt, j_ptsb, j_o, j_g = (
        sem(x) for x in ("job_scores", "job_max", "job_exp", "job_probs", "job_pT", "job_pT_sb", "job_out", "job_gated"))
    g_f, g_ln, g_d, g_e, g_w, g_vt, g_vsb, g_kt, g_ksb = (
        sem(x) for x in ("hg_f", "hg_ln", "hg_diff", "hg_exp", "hg_weighted", "hg_vT", "hg_v", "hg_kT", "hg_k"))
    g_sc, g_st, g_u, g_s, g_o, g_osq, g_sum, g_ms, g_y, g_g, g_x = (
        sem(x) for x in ("hg_scores", "hg_masked", "hg_update", "hg_state", "hg_out", "hg_outsq", "hg_sum", "hg_mean",
                         "hg_rsqrt", "hg_gated", "hg_samples"))
    s0_in, hs_out, g_vz = [sem("s0_landed0"), sem("s0_landed1")], sem("state_stored"), sem("hg_vz")
    e_u, e_cs, e_cst, e_cso, cs_out = sem("u_ready"), sem("cin_ready"), sem("cs_transposed"), sem("cs_evac"), None
    e_z, e_y, e_yh = sem("z1_sigmoid"), sem("y_f32"), sem("y_hi")
    f_x, f_t, f_e, y_out = sem("x2_ready"), sem("x2_transposed"), sem("y_evac"), sem("y_stored")
    passthru = sem("cache_copied")

    def wview(w):
        return w.rearrange("(k p) n -> p k n", p=P)

    w_in0, w_out0 = wview(a["even_w_in"][0]), wview(a["even_w_out"][0])
    w_in1, w_out1 = wview(a["odd_w_in"][0]), wview(a["odd_w_out"][0])
    w_ada = [wview(a["ada_w"][n]) for n in range(2)]

    B = UC
    phases = [
        ("kv", U_KV, 1, w_in0, lambda i: 4 * B, 0, None),
        ("q", U_Q, 2, w_in0, lambda i: 2 * i * B, 0, 16),
        ("qb", U_QB, 2, w_in0, lambda i: 10 * B + 2 * i * B, 0, 20),
        ("f", U_F, 2, w_in0, lambda i: 14 * B + 2 * i * B, 0, 24),
        ("i", U_I, 2, w_in0, lambda i: 18 * B + 2 * i * B, 0, 28),
        ("za", U_ZA, 2, w_in0, lambda i: 6 * B + 2 * i * B, 0, 32),
        ("zb", U_ZB, 2, w_in0, lambda i: 22 * B + 2 * i * B, 0, 36),
    ]

    def loop(eng, n, body, *steps):
        if n == 1:
            body(0)
            return
        with eng.Fori(0, n) as i:
            for s, per in steps:
                s.enter(i, per)
            body(i)
        for s, _ in steps:
            s.leave(n)

    ynat = scratch("ynat", [P, 3, D], 0)
    csn = soft[0:48, 0:UC]

    cst = sb("cst", [P, 2, 18], F32, o_acts + 52 * T * 4)
    u_sb = acts[:, 53:55, :]
    gc = acts[:, 55:57, :]
    sz = acts[:, 57:59, :]
    cin = acts[:, 16:20, :].rearrange("p c t -> p (c t)")[:, 0:2 * 338].rearrange("p (m t) -> p m t", m=2)
    cv = norm[:, 0:2 * 336].rearrange("p (m t) -> p m t", m=2)
    xo = [acts[:, 16:18, :], acts[:, 18:20, :]]
    gtmp = stmp[:, :].rearrange("p (m t) -> p m t", m=2)

    def hgrn_store(pool, h):
        pool.wait_ge(g_s, 4 * h + 4)
        pool.dma_start(o["sh_p"][0, 0, h], sst[:, 3]).then_inc(hp_out, 16)
        pool.wait_ge(g_x, h + 1)
        pool.dma_start(o["sh_s"][0, :, h].rearrange("b k v -> k b v"), s0[:, h % 2]).then_inc(hs_out, 16)

    block = ctx.enter_context(nc.Block())

    @block.sync
    def _(sp):
        sp.dma_start(cnat[0:1, 0, :], a["c_prompt"]).then_inc(s_cin, 16)
        sp.dma_start(cnat[1:NSEQ, 0, :], a["c_sample"]).then_inc(s_cin, 16)
        sp.dma_start(vnat1[:, 0, :], a["ada_b"].rearrange("l (c p) -> (l c) p", p=P)).then_inc(s_vec, 16)
        sp.dma_start(vnat2[0:32, 0, :], a["norm_w"].rearrange("l (c p) -> (l c) p", p=P)).then_inc(s_vec, 16)
        sp.dma_start(vnat2[32:80, 0, :], a["odd_conv_w"].rearrange("l i (c p) -> (l i c) p", p=P)).then_inc(s_vec, 16)
        sp.dma_start(vnat2[80:88, 0, :], a["hgrn_lb_logits"].rearrange("l (c p) -> (l c) p", p=P)).then_inc(s_vec, 16)
        for n, name in ((0, "q_norm_w"), (1, "k_norm_w")):
            for half in range(2):
                sp.dma_start(vnat2[88 + n:89 + n, 0, 64 * half:64 * half + 64], a[name]).then_inc(s_vec, 16)
        sp.dma_start(vnat2[90:91, 0, :], a["hgrn_norm_w"]).then_inc(s_vec, 16)
        for t in range(2):
            sp.dma_start(xnat[:, t, :], a["x_prompt"][0, t * P:(t + 1) * P, :]).then_inc(s_xin, 16)
        sp.dma_start(xnat[0:NS, 2, :], a["x_sample"].rearrange("b j d -> (b j) d")).then_inc(s_xin, 16)
        sp.dma_start(scnat[:, 0, :], a["state_conv"].rearrange("l b r d -> (l b r) d")).then_inc(s_scin, 16)

        def load_ada(G, col, layer):
            for s in range(4):
                sp.wait_ge(ada_used, 4 * G - 3 + s)
                sp.dma_start(adaw[:, s], w_ada[layer][:, QK * s:QK * s + QK, ds(col, UC)]).then_inc(s_aq[s], 16)

        def load_ada_pair(i):
            for e, (buf, landed) in enumerate(((adaw, s_aq), (adaw2, s_aq2))):
                for s in range(4):
                    if not (isinstance(i, int) and i == 0):
                        sp.wait_ge(ada_used, 8 * i + 4 * e - 7 + s)
                    sp.dma_start(buf[:, s], w_ada[0][:, QK * s:QK * s + QK, ds((2 * i + e) * UC, UC)])\
                        .then_inc(landed[s], 16)

        def load_unit(U, w, col, wait=True):
            for q in range(4):
                if wait:
                    sp.wait_ge(lo_ready, 4 * U + q - 3)
                sp.dma_start(raw[:, q], w[:, QK * q:QK * q + QK, ds(col, UC)]).then_inc(s_wq[q], 16)

        load_ada_pair(0)
        with sp.Fori(1, GA // 2) as i:
            load_ada_pair(i)
        for name, U0, n, w, col, _, G0 in phases:
            def body(i):
                for p in range(2):
                    U = U0 + 2 * i + p
                    if G0 is not None:
                        g = G0 if G0 < 24 else G0 - 24
                        load_ada(G0 + 2 * i + p, (g + 2 * i + p) * UC, G0 // 24)
                    load_unit(U, w, col(i) + p * UC, name != "kv" or p > 0)
            loop(sp, n, body)

        def out0(i):
            for p in range(2):
                load_unit(U_OUT0 + 2 * i + p, w_out0, (2 * i + p) * UC)
        loop(sp, 4, out0)

        def in1(i):
            load_ada(40 + i, (16 + i) * UC, 1)
            for k, part in enumerate((0, 1, 2, 3)):
                load_unit(U_IN1 + 4 * i + k, w_in1, part * D + i * UC)
        loop(sp, 8, in1)

        def out1(i):
            for p in range(2):
                load_unit(U_OUT1 + 2 * i + p, w_out1, (2 * i + p) * UC)
        loop(sp, 4, out1)

    @block.gpsimd
    def _(pool):
        g = nc.gpsimd
        steps = Steps(pool, pool_s)

        def st(ins):
            steps(ins)
            steps.settle()

        def select(out, pattern, base, mult, op, fill):
            st(g.affine_select(out=out, in_=out, compare_op=op, fill=fill, base=base, pattern=pattern,
                               channel_multiplier=mult))

        st(g.memset(ident[:], 0.0))
        select(ident[:], [[-1, P]], 0, 1, ALU.not_equal, 1.0)
        st(g.memset(cond[:], 0.0))
        st(g.memset(sel[:], 0.0))
        for j in range(4):
            select(sel[:], [[-1, NSEQ]], -32 * j, 1, ALU.not_equal, 1.0)
        g.memset(ones[:], 1.0).then_inc(consts, 1)
        pool.wait_ge(consts, 1)
        st(g.memset(blk[:], 0.0))
        st(g.memset(seqm[:], 1.0))
        st(g.memset(rmask[:], 1.0))
        st(g.memset(lmask[:], 0.0))
        st(g.memset(pmask[:], 0.0))
        st(g.memset(m8[:, 0, :], -1e30))
        st(g.memset(rep8[:], 0.0))
        m8v = m8[:, 0, :]
        st(g.memset(m8v[:, 0:WIN], 0.0))
        st(g.memset(m8v[:, WIN:].rearrange("p (n c) -> p n c", c=72)[:, :, 0:NJ], 0.0))
        select(m8v[:, 0:WIN], [[1, WIN]], 0, -1, ALU.is_ge, -1e30)
        select(m8v[:, WIN:].rearrange("p (n c) -> p n c", c=72)[:, :, 0:NJ], [[0, NB], [-1, NJ]], 0, 1, ALU.is_ge, -1e30)
        select(rep8[:].rearrange("p (n j) -> p n j", j=NJ), [[0, 16], [-1, NJ]], 0, 1, ALU.not_equal, 1.0)
        st(g.memset(blk[0:64, 0:64], 1.0))
        g.memset(blk[64:128, 64:128], 1.0).then_inc(consts, 1)
        pool.wait_ge(consts, 2)
        st(g.memset(rmask[:, 0:SEQ].rearrange("p (n c) -> p n c", c=64)[:, :, 0:1], 0.0))
        st(g.memset(rmask[:, SEQ:T].rearrange("p (n c) -> p n c", c=NJ)[:, :, 0:1], 0.0))
        for l, h in enumerate(LEVELS):
            st(g.memset(lmask[0:64, l, :].rearrange("p (n e h) -> p n e h", e=2, h=h)[:, :, 1, :], 1.0))
        select(seqm[:], [[-NJ, NB]], 0, 1, ALU.is_ge, 0.0)
        select(seqm[:], [[NJ, NB]], NJ - 1, -1, ALU.is_ge, 0.0)
        for l, h in enumerate(LEVELS):
            v = lmask[0:64, l, :].rearrange("p (n e h) -> p n e h", e=2, h=h)
            n = 64 // (2 * h)
            select(v, [[-2 * h, n], [0, 2], [0, h]], 0, 1, ALU.is_ge, 0.0)
            select(v, [[2 * h, n], [0, 2], [0, h]], h - 1, -1, ALU.is_ge, 0.0)
        select(lmask[0:64, NL, :], [[-1, 64]], 0, 1, ALU.not_equal, 1.0)
        select(pmask[:, 0:128], [[-1, 128]], 0, 1, ALU.is_ge, -1e30)
        select(pmask[:, 128:384], [[1, 256]], 0, -1, ALU.is_ge, -1e30)
        select(pmask[:, 128:384], [[-1, 256]], WIN, 1, ALU.is_ge, -1e30)
        pool.dma_start(lmask[64:128], lmask[0:64]).then_inc(s_cst, 16)
        pool.dma_start(sinkp[:, :], a["attn_sinks"][0:1, :].partition_broadcast(P)).then_inc(s_cst, 16)
        with nc.allow_non_contiguous_dma("128 sink values, once"):
            pool.dma_start(sinks[:, :], a["attn_sinks"][0, :][:, None].to_broadcast([HEADS, NJ])).then_inc(s_cst, 16)
        for n, (src, dst) in enumerate((("cache_k", "ck_s"), ("cache_v", "cv_s"))):
            pool.dma_start(o[dst][0, :, 0:WIN - NJ].rearrange("b s k d -> b (s k d)"),
                           a[src][0, :, NJ:WIN].rearrange("b s k d -> b (s k d)")).then_inc(passthru, 16)
        pool.wait_ge(xc_act, KC)
        pool.dma_start(xspill, acts[:, C_X0:C_X0 + KC, :].rearrange("p c t -> p (c t)")).then_inc(stored, 16)
        pool.wait_ge(quarter_used, 4 * U_OUT0)
        pool.dma_start(ckn[:], a["cache_k"][0].rearrange("b s k d -> s b (k d)")).then_inc(cache_in, 16)
        pool.dma_start(vc[:], a["cache_v"][0].rearrange("b s k d -> s b (k d)")).then_inc(cache_in, 16)
        pool.wait_ge(t_sb, 3)
        for n, (src, dp, dst) in enumerate(((knat, "ck_p", "ck_s"), (vnat, "cv_p", "cv_s"))):
            pool.dma_start(o[dp][0, 0].rearrange("s k d -> s (k d)"), src[:, 1, :]).then_inc(kv_out, 16)
            for b in range(NB):
                pool.dma_start(o[dst][0, b, WIN - NJ:WIN].rearrange("s k d -> s (k d)"),
                               src[NJ * b:NJ * b + NJ, 2, :]).then_inc(kv_out, 16)
        pool.wait_ge(j_g, 20)
        pool.wait_ge(kv_out, 16 * 18)
        def load_states(h):
            if h >= 2:
                pool.wait_ge(hs_out, 16 * (h - 1))
            pool.dma_start(s0[:, h % 2], a["state_hgrn"][0, :, h].rearrange("b k v -> k b v")).then_inc(s0_in[h % 2], 16)

        load_states(0)
        load_states(1)
        for h in range(HH):
            pool.wait_ge(g_vsb, h + 1)
            if h >= 1:
                pool.wait_ge(g_u, 3 * h)
            for bb in range(NB):
                last = g.tensor_scalar(vz[:, bb, :], vn[0:NS, 2, :], seqm[:, bb:bb + 1], None, ALU.mult)
                if bb == NB - 1:
                    last.then_inc(g_vz, 1)
                else:
                    st(last)
            if h >= 1:
                hgrn_store(pool, h - 1)
                if h + 1 < HH:
                    load_states(h + 1)
        hgrn_store(pool, HH - 1)
        pool.wait_ge(g_g, HH)
        pool.wait_ge(stored, 16)
        pool.dma_start(acts[:, C_X1:C_X1 + KC, :].rearrange("p c t -> p (c t)"), xspill).then_inc(x1_loaded, 16)
        def conv_state_out(i):
            pool.wait_ge(e_cso, i + 1)
            pool.dma_start(o["sc_p"][0, 0][:, ds(i * UC, UC)], csn[0:2]).then_inc(stored, 16)
            pool.dma_start(o["sc_s"][0].rearrange("b r d -> (b r) d")[:, ds(i * UC, UC)], csn[32:48]).then_inc(stored, 16)
        loop(pool, 8, conv_state_out)
        for u in range(8):
            pool.wait_ge(f_e, u + 1)
            c = slice(u * UC, u * UC + UC)
            for t in range(2):
                pool.dma_start(o["y_p"][0, t * P:(t + 1) * P, c], ynat[:, t, c]).then_inc(y_out, 16)
            pool.dma_start(o["y_s"].rearrange("b j d -> (b j) d")[:, c], ynat[0:NS, 2, c]).then_inc(y_out, 16)
        pool.wait_ge(y_out, 16 * 24)
        pool.wait_ge(stored, 16 * 17)
        pool.wait_ge(hs_out, 16 * HH)
        pool.wait_ge(hp_out, 16 * HH)
        pool.wait_ge(kv_out, 16 * 18)
        pool.wait_ge(passthru, 32)

    @block.tensor
    def _(pe):
        mm, tr = nc.tensor.matmul, nc.tensor.transpose

        def unit(U, par, oph, opl, opset):
            b0 = 2 * par
            first = not isinstance(U, int) or U >= 2
            if first:
                if isinstance(U, int):
                    pe.wait_ge(bank_free[par], U // 2)
                else:
                    pe.wait_ge(bank_free[par], U[0])
            base = U if isinstance(U, int) else U[1]
            for q in range(4):
                pe.wait_ge(lo_ready, 4 * base + q + 1)
                pe.wait_ge(h_ready, KC * opset + QK * q + QK)
                for m in range(2):
                    for k in range(QK):
                        kk = QK * q + k
                        out = pproj[:, b0 + m, 0:T]
                        cs = slice(m * P, m * P + P)
                        mm(out, wh[:, q, k, cs], oph[:, kk, :], start=(kk == 0), stop=False)
                        mm(out, wh[:, q, k, cs], opl[:, kk, :], start=False, stop=False)
                        last = mm(out, wl[:, q, k, cs], oph[:, kk, :], start=False, stop=(kk == KC - 1))
                last.then_inc(quarter_used, 1)

        def ada_accumulate(G, landed, first=False, buf=adaw, sems=s_aq):
            if not first:
                pe.wait_ge(ada_out, G)
            for s in range(4):
                pe.wait_ge(sems[s], landed)
                for j in range(4):
                    last = mm(bank[0][32 * j:32 * j + 32, 0:UC], cond[:, QK * s + j, :], buf[:, s, j, :],
                              start=(s == 0), stop=(s == 3), skip_group_check=True)
                last.then_inc(ada_used, 1)

        def ada_select(G, first=False):
            pe.wait_ge(ada_out, G + 1)
            if not first:
                pe.wait_ge(mod_done, G)
            for m in range(2):
                last = mm(bank[1][:, NSEQ * m:NSEQ * m + NSEQ], adas[:, m * P:m * P + P], sel[:],
                          start=True, stop=True)
            last.then_inc(ada_sel, 1)

        pe.wait_ge(consts, 1)
        pe.wait_ge(s_cin, 32)
        for c in range(KC):
            last = tr(bank[0][:, NSEQ * c:NSEQ * c + NSEQ], cnat[0:NSEQ, 0, c * P:c * P + P], ident[0:NSEQ, 0:NSEQ])
        last.then_inc(s_tp, 1)
        pe.wait_ge(s_vec, 16 * 9)
        tr(bank[1][:, 0:96], vnat1[:, 0, :], ident[0:96, 0:96])
        tr(bank[1][:, 96:96 + 91], vnat2[:, 0, :], ident[0:91, 0:91]).then_inc(s_tp, 1)
        pe.wait_ge(s_scin, 16)
        for c in range(KC):
            last = tr(bank[2][:, 16 * c:16 * c + 16], scnat[:, 0, c * P:c * P + P], ident[0:16, 0:16])
        last.then_inc(s_tp, 1)
        pe.wait_ge(s_xin, 48)
        for c in range(KC):
            if c >= 2:
                pe.wait_ge(xc_act, c - 1)
            else:
                pe.wait_ge(s_tpe, 3)
            for t in range(3):
                r = P if t < 2 else NS
                last = tr(bank[2 + c % 2][:, t * P:t * P + r], xnat[0:r, t, c * P:c * P + P], ident[0:r, 0:r])
            last.then_inc(s_tp, 1)

        def norm_sum(layer):
            pe.wait_ge(ss_done, layer + 1)
            pe.wait_ge(xc_act, KC)
            mm(bank[2][:, 0:T], ones[:], ssq, start=True, stop=True).then_inc(ss_sum, 1)

        pe.wait_ge(cond_done, 1)
        ada_accumulate(0, 16, True)
        pe.wait_ge(consts, 2)
        pe.wait_ge(xc_act, KC)
        mm(bank[3][:, 0:WIN], rep8[:], m8[:, 0, 0:WIN], start=True, stop=True).then_inc(s_tp, 1)
        pe.wait_ge(s_tpe, 4)
        mm(bank[3][:, 0:512], rep8[:], m8[:, 0, WIN:WIN + 512], start=True, stop=True).then_inc(s_tp, 1)
        norm_sum(0)
        ada_select(0, True)
        ada_accumulate(1, 16, buf=adaw2, sems=s_aq2)
        ada_select(1)
        with pe.Fori(1, GA // 2) as i:
            ada_accumulate(2 * i, 16 * i + 16)
            ada_select(2 * i)
            ada_accumulate(2 * i + 1, 16 * i + 16, buf=adaw2, sems=s_aq2)
            ada_select(2 * i + 1)

        def head_sums(s):
            pe.wait_ge(n_sq, s + 1)
            if not (isinstance(s, int) and s == 0):
                pe.wait_ge(n_ms, s)
            for m in range(2):
                last = mm(bank[2 + m][:, 0:T], blk[:], soft[:, m * T:m * T + T], start=True, stop=True)
            last.then_inc(n_sum, 1)

        for name, U0, n, w, col, opset, G0 in phases:
            def body(i):
                for p in range(2):
                    if G0 is not None:
                        ada_accumulate(G0 + 2 * i + p, 16 * (G0 + 2 * i + p - GA // 2 + 1))
                    if isinstance(i, int):
                        unit(U0 + 2 * i + p, p, hh, hl, opset)
                    else:
                        unit((i + U0 // 2, i * 2 + U0 + p), p, hh, hl, opset)
                    if G0 is not None:
                        ada_select(G0 + 2 * i + p)
                    if name == "qb":
                        head_sums(2 * i + p + 1)
            loop(pe, n, body)
            if name == "q":
                head_sums(0)

        sc_ps = [bank[2], bank[3], pproj[:, 0, :]]
        pt_ps = [bank[0], pproj[:, 2, :]]
        o_ps = [bank[1], pproj[:, 3, :]]
        pe.wait_ge(bank_free[0], U_OUT0 // 2)
        pe.wait_ge(bank_free[1], U_OUT0 // 2)
        pe.wait_ge(mod_done, 40)
        pe.wait_ge(n_q, 5)
        pe.wait_ge(k_sw, 1)

        def scores(j):
            if j >= 3:
                pe.wait_ge(j_max, j - 2)
            ps = sc_ps[j % 3]
            if j < HEADS:
                kv, rows = j // 4, slice(64 * (j % 2), 64 * (j % 2) + 64)
                q = acts[rows, C_Q + j // 2, :]
                k = acts[rows, C_K + kv // 2, :] if kv % 2 == j % 2 else ksw[rows, kv // 2, :]
                mm(ps[:, 0:128], q[:, 0:128], k[:, 0:128], start=True, stop=True)
                last = mm(ps[:, 128:384], q[:, 128:256], k[:, 0:256], start=True, stop=True)
            else:
                pe.wait_ge(c_sb, j - HEADS + 1)
                pe.wait_ge(q_st, 1)
                for e in range(2):
                    b = 2 * (j - HEADS) + e
                    for kv in range(KVH):
                        kc, rows = kv // 2, slice(64 * (kv % 2), 64 * (kv % 2) + 64)
                        qs = qs2[rows, kc, b, :, :].rearrange("p r j -> p (r j)")
                        out = ps[32 * kv:32 * kv + 32, 192 * e:192 * e + 192]
                        mm(out[:, 0:WIN], qs, kct[rows, b, kc, :], start=True, stop=True)
                        last = mm(out[:, WIN:192], qs, acts[rows, C_K + kc, SEQ:T], start=True, stop=True)
            last.then_inc(j_sc, 1)

        def probs_t(j):
            pe.wait_ge(j_p, j + 1)
            if j >= 2:
                pe.wait_ge(j_ptsb, j - 1)
            pj, ps = p4[:, j % 4, :], pt_ps[j % 2]
            if j < HEADS:
                for k in range(3):
                    last = tr(ps[:, k * P:k * P + P], pj[:, k * P:k * P + P], ident[:])
            else:
                for e in range(2):
                    tr(ps[:, e * P:e * P + P], pj[:, 192 * e:192 * e + WIN], ident[:])
                    last = tr(ps[0:NS, 256 + e * P:256 + e * P + P], pj[:, 192 * e + WIN:192 * e + 192], ident[:])
            last.then_inc(j_pt, 1)

        def outputs(j):
            pe.wait_ge(j_ptsb, j + 1)
            if j >= 2:
                pe.wait_ge(j_g, j - 1)
            pt, ps = pt2[:, j % 2, :], o_ps[j % 2]
            if j < HEADS:
                kv = j // 4
                rows = slice(64 * (j % 2), 64 * (j % 2) + 64)
                vs = slice(64 * kv, 64 * kv + 64)
                mm(ps[rows, 0:128], vnat[:, 0, vs], pt[:, 0:128], start=True, stop=True)
                mm(ps[rows, 128:256], vnat[:, 0, vs], pt[:, 128:256], start=True, stop=False)
                last = mm(ps[rows, 128:256], vnat[:, 1, vs], pt[:, 256:384], start=False, stop=True)
            else:
                for e in range(2):
                    b = 2 * (j - HEADS) + e
                    for kv in range(KVH):
                        vs = slice(64 * kv, 64 * kv + 64)
                        out = ps[0:64, P * e + 32 * kv:P * e + 32 * kv + 32]
                        mm(out, vc[:, b, vs], pt[:, e * P + 32 * kv:e * P + 32 * kv + 32], start=True, stop=False)
                        last = mm(out, vnat[0:NS, 2, vs], pt[0:NS, 256 + e * P + 32 * kv:256 + e * P + 32 * kv + 32],
                                  start=False, stop=True)
            last.then_inc(j_o, 1)

        def cached_keys(g):
            if g == 0:
                pe.wait_ge(cache_in, 32)
            else:
                pe.wait_ge(c_sb, g)
            for k in range(4):
                b, kc = 2 * g + k // 2, k % 2
                last = tr(pproj[:, 1, k * P:k * P + P], ckn[:, b, kc * P:kc * P + P], ident[:])
            last.then_inc(c_ps, 1)

        for j in range(3):
            scores(j)
        for t, ps in enumerate((bank[0], bank[1], pproj[:, 3, :])):
            r = P if t < 2 else NS
            for kc in range(2):
                tr(ps[0:r, kc * P:kc * P + P], acts[:, C_K + kc, t * P:t * P + r], ident[:])
                last = tr(ps[0:r, 256 + kc * P:256 + kc * P + P], acts[:, C_V + kc, t * P:t * P + r], ident[:])
            last.then_inc(t_ps, 1)
        pe.wait_ge(t_sb, 3)
        for j in range(20):
            probs_t(j)
            if 4 <= j < 8:
                cached_keys(j - 4)
            if j + 3 < 20:
                scores(j + 3)
            if j >= 1:
                outputs(j - 1)
        outputs(19)

        pe.wait_ge(j_g, 20)
        pe.wait_ge(bank_free[0], U_OUT0 // 2)
        pe.wait_ge(bank_free[1], U_OUT0 // 2)

        def hgrn_scores(h):
            hbuf = hbufs[h % 2]
            if h >= 1:
                pe.wait_ge(g_ksb, h)
            for t in range(3):
                r = P if t < 2 else NS
                last = tr(bank[3][0:r, t * P:t * P + P], acts[:, C_I + h, t * P:t * P + r], ident[:])
            last.then_inc(g_vt, 1)
            if h >= 1:
                pe.wait_ge(g_st, h)
            pe.wait_ge(g_w, h + 1)
            W = hbuf[:, 0:NL * SEQ].rearrange("p (l t) -> p l t", l=NL)
            WS = hbuf[:, NL * SEQ:NL * SEQ + 3 * NS].rearrange("p (l t) -> p l t", l=3)
            kk, qq = acts[:, C_KB + h, :], acts[:, C_QB + h, :]
            for c in range(4):
                out = bank[c // 2][64 * (c % 2):64 * (c % 2) + 64, :]
                t = slice(64 * c, 64 * c + 64)
                for l in range(NL):
                    mm(out[:, 64 * l:64 * l + 64], W[:, l, t], W[:, l, t], start=True, stop=True)
                mm(out[:, 64 * NL:64 * NL + 64], kk[:, t], qq[:, t], start=True, stop=True)
            for l in range(3):
                mm(bank[2][0:64, 64 * l:64 * l + 64], WS[:, l, :], WS[:, l, :], start=True, stop=True)
            mm(bank[2][0:64, 192:256], kk[:, SEQ:T], qq[:, SEQ:T], start=True, stop=True).then_inc(g_sc, 1)
            pe.wait_ge(g_vsb, h + 1)
            ke = hbuf[:, 2048:2368]
            for t in range(3):
                r = P if t < 2 else NS
                last = tr(bank[3][0:r, t * P:t * P + P], ke[:, t * P:t * P + r], ident[:])
            last.then_inc(g_kt, 1)

        hgrn_scores(0)
        for h in range(HH):
            qeb = qebs[h % 2]
            pe.wait_ge(g_ksb, h + 1)
            if h >= 1:
                pe.wait_ge(g_s, 4 * h)
            for half in range(2):
                rows = slice(64 * half, 64 * half + 64)
                for t in range(2):
                    c = 2 * t + half
                    last = mm(pproj[:, 0, c * P:c * P + P], ken[rows, t, :], vn[rows, t, :], start=True, stop=True)
                last.then_inc(g_u, 1)
                pe.wait_ge(g_u, 3 * h + half + 1)
            pe.wait_ge(g_vz, h + 1)
            if h >= 1:
                pe.wait_ge(g_x, h)
            for e in range(2):
                last = mm(pproj[:, 1 + e, :], ken[0:NS, 2, :], vz[:, 4 * e:4 * e + 4, :], start=True, stop=True)
            last.then_inc(g_u, 1)
            pe.wait_ge(g_st, h + 1)
            pe.wait_ge(s0_in[h % 2], 16 * (h // 2) + 16)
            if h >= 1:
                pe.wait_ge(g_ms, h)
            mm(pproj[:, 3, SEQ:T], vn[0:NS, 2, :], stt_[0:NS, 2, :], start=True, stop=False)
            for b in range(NB):
                c = slice(SEQ + NJ * b, SEQ + NJ * b + NJ)
                last = mm(pproj[:, 3, c], s0[:, h % 2, b, :], qeb[:, c], start=False, stop=(b == NB - 1))
            last.then_inc(g_o, 1)
            for c in range(4):
                rows, t = slice(64 * (c % 2), 64 * (c % 2) + 64), c // 2
                out = pproj[:, 3, 64 * c:64 * c + 64]
                if c:
                    pe.wait_ge(g_s, 4 * h + c)
                    mm(out, sst[:, c - 1, :], qeb[:, 64 * c:64 * c + 64], start=True, stop=False)
                pe.wait_ge(g_o, 5 * h + c + 1)
                mm(out, vn[rows, t, :], stt_[rows, t, :], start=(c == 0), stop=True).then_inc(g_o, 1)
            pe.wait_ge(g_osq, h + 1)
            mm(pproj[:, 3, 0:T], ones[:], osq[:], start=True, stop=True).then_inc(g_sum, 1)
            if h + 1 < HH:
                hgrn_scores(h + 1)

        def out0(i):
            for p in range(2):
                unit((i + U_OUT0 // 2, i * 2 + U_OUT0 + p), p, hh, hl, 1)
        loop(pe, 4, out0)
        norm_sum(1)

        def in1(i):
            ada_accumulate(40 + i, 16 * (41 - GA // 2 + i))
            for k in range(4):
                U = U_IN1 + 4 * i + k
                unit((i * 2 + (U_IN1 + k) // 2, U), k % 2, hh, hl, 2)
            ada_select(40 + i)
            pe.wait_ge(e_cs, 2 * i + 2)
            for m in range(2):
                tr(bank[2][0:2, m * P:m * P + P], cst[:, m, 0:2], ident[:])
                last = tr(bank[3][0:16, m * P:m * P + P], cst[:, m, 2:18], ident[:])
            last.then_inc(e_cst, 1)
        loop(pe, 8, in1)

        def y_rows(u, par):
            pe.wait_ge(f_x, u + 1)
            if not (isinstance(u, int) and u == 0):
                pe.wait_ge(f_e, u)
            for m in range(2):
                for t in range(3):
                    r = P if t < 2 else NS
                    last = tr(bank[t][0:r, m * P:m * P + P], xo[par][:, m, t * P:t * P + r], ident[:])
            last.then_inc(f_t, 1)

        def out1(i):
            first = isinstance(i, int) and i == 0
            for p in range(2):
                unit((i + U_OUT1 // 2, i * 2 + U_OUT1 + p), p, yh, yl, 3)
                if not (first and p == 0):
                    y_rows(2 * i + p - 1, 1 - p)
        out1(0)
        with pe.Fori(1, 3) as i:
            out1(i)
        out1(3)
        y_rows(7, 1)

    @block.scalar
    def _(act):
        A = nc.scalar.activation
        st = Steps(act, act_s)

        def split_hi(U, q):
            act.wait_ge(s_wq[q], 16 * U + 16)
            if not isinstance(U, int) or U > 0:
                act.wait_ge(quarter_used, 4 * U + q - 3)
            A(wh[:, q], raw[:, q], ACT.Copy).then_inc(hi_ready, 1)

        def around(U, evac, last=False):
            if not last:
                for q in range(3):
                    split_hi(U + 1, q)
            if evac:
                act.wait_ge(quarter_used, 4 * U + 4)
                act.wait_ge(hi_ready, 4 * U + 7)
                evac()
            if not last:
                split_hi(U + 1, 3)

        def ada_evac(G, first=False):
            act.wait_ge(ada_used, 4 * G + 4)
            if not first:
                act.wait_ge(ada_sel, G)
            A(adas[:], bank[0][:, 0:UC], ACT.Copy).then_inc(ada_out, 1)

        act.wait_ge(s_tp, 1)
        A(soft[:, 0:KC * NSEQ], bank[0][:, 0:KC * NSEQ], ACT.Sigmoid).then_inc(csig, 1)
        act.wait_ge(s_tp, 2)
        A(vecs[:, 0:187], bank[1][:, 0:187], ACT.Copy).then_inc(vecs_done, 1)
        act.wait_ge(s_tp, 3)
        A(sct[:], bank[2][:, 0:256].rearrange("p (c r) -> p c r", c=KC), ACT.Copy).then_inc(s_tpe, 3)
        for c in range(KC):
            act.wait_ge(s_tp, 4 + c)
            ps = bank[2 + c % 2][:, 0:T]
            if c >= 2:
                act.wait_ge(sqr, c)
            A(xsq[:, c % 2, :], ps, ACT.Square).then_inc(h_sq, 1)
            A(acts[:, C_X0 + c, :], ps, ACT.Copy).then_inc(xc_act, 1)
        ada_evac(0, True)
        act.wait_ge(s_tp, 4 + KC)
        A(smask[:, 0:WIN], bank[3][:, 0:WIN], ACT.Copy).then_inc(s_tpe, 1)
        act.wait_ge(s_tp, 5 + KC)
        A(smask[:, WIN:WIN + 512], bank[3][:, 0:512], ACT.Copy).then_inc(s_tpe, 1)

        def rsqrt(out, in_):
            st(A(out, in_, ACT.Ln))
            st.settle()
            return A(out, out, ACT.Exp, scale=-0.5)

        def token_rsqrt(layer):
            act.wait_ge(ms_ready, layer + 1)
            rsqrt(rstd, hb[:, 0, :]).then_inc(rs_ready, 1)

        def modulate(layer, j, par):
            n = KC // 2 * layer + j + 1
            h = hbs[par]
            act.wait_ge(h_nrm, n)
            for e in range(2):
                sh = mods[:, ds(48 * layer + 2 * j + e, 1), 0:1].rearrange("p c s -> p (c s)")
                s1c = s1[:, ds(2 * j + e, 1), 0:1].rearrange("p c s -> p (c s)")
                last = A(h[:, e, 0:SEQ], h[:, e, 0:SEQ], ACT.Identity, bias=sh, scale=s1c)
            last.then_inc(h_aff, 1)
            act.wait_ge(hb_ready, n)
            act.wait_ge(h_aff, n)
            A(hh[:, ds(2 * j, 2), :], h, ACT.Copy).then_inc(h_hi, 1)

        def head_squares(x, s):
            if not (isinstance(s, int) and s == 0):
                act.wait_ge(n_q, s)
            A(soft[:, 0:2 * T].rearrange("p (m t) -> p m t", m=2), x, ACT.Square).then_inc(n_sq, 1)

        def head_rsqrt(s):
            act.wait_ge(n_ms, s + 1)
            act_y = soft[:, 2 * T:4 * T]
            rsqrt(act_y, soft[:, 0:2 * T]).then_inc(n_y, 1)

        nc.scalar.preload_act_table_set("natural_log_exp_and_others")
        token_rsqrt(0)
        ada_evac(1)
        with act.Fori(1, GA // 4) as i:
            ada_evac(2 * i)
            ada_evac(2 * i + 1)
        with act.Fori(GA // 4, GA // 2) as i:
            for e in range(2):
                ada_evac(2 * i + e)
                modulate(0, 2 * i + e - GA // 2, e)
        for q in range(4):
            split_hi(0, q)
        for name, U0, n, w, col, opset, G0 in phases:
            def body(i):
                for p in range(2):
                    U = U0 + 2 * i + p
                    if G0 is not None:
                        ada_evac(G0 + 2 * i + p)
                    if name == "qb":
                        head_squares(acts[:, ds(C_Q + 4 * i + 2 * p, 2), :], 2 * i + p + 1)
                    ps = pproj[:, 2 * p:2 * p + 2, 0:T]

                    def store(c, scale=1.0):
                        A(acts[:, ds(c + 4 * i + 2 * p, 2), :], ps, ACT.Copy, scale=scale).then_inc(bank_free[p], 1)

                    def evac():
                        if name == "kv":
                            A(acts[:, C_K + 2 * p:C_K + 2 * p + 2, :], ps, ACT.Copy).then_inc(bank_free[p], 1)
                        elif name == "q":
                            store(C_Q)
                        elif name == "qb":
                            store(C_QB, float(DK) ** -0.5)
                        elif name == "i":
                            store(C_I)
                        elif name == "f":
                            A(acts[:, ds(C_S + 4 * i + 2 * p, 2), :], ps, ACT.Sigmoid)
                            A(acts[:, ds(C_KB + 4 * i + 2 * p, 2), :], ps, ACT.Sigmoid, scale=-1.0)\
                                .then_inc(bank_free[p], 1)
                        else:
                            act.wait_ge(bank_free[1 - p], i + U0 // 2 + p)
                            A(hb, ps, ACT.Sigmoid).then_inc(z_sig, 1)
                        if name == "qb":
                            head_rsqrt(2 * i + p + 1)
                    around(U, evac)
            loop(act, n, body, *(((st, 2),) if name == "qb" else ()))
            if name == "kv":
                head_squares(acts[:, C_K:C_K + 2, :], 0)
            if name == "q":
                head_rsqrt(0)

        nc.scalar.preload_act_table_set("natural_log_exp_and_others")
        act.wait_ge(lb_exp, 1)
        A(lb[:, 1, :], lb[:, 0, :], ACT.Exp).then_inc(lb_exp, 1)
        act.wait_ge(k_sw, 1)

        def exps(j):
            act.wait_ge(j_max, j + 1)
            c = 128 if j < HEADS else 192
            pj = p4[:, j % 4, :]
            nm = stmp[:, 8 * (j % 4):8 * (j % 4) + 8]
            sk = sinkp[:, j:j + 1] if j < HEADS else sinks[:, 0:1]
            A(pj[:, 0:c], pj[:, 0:c], ACT.Exp, bias=nm[:, 0:1], accum_out=nm[:, 2:3])
            A(pj[:, c:384], pj[:, c:384], ACT.Exp, bias=nm[:, 1:2], accum_out=nm[:, 3:4])
            A(nm[:, 4:6], nm[:, 0:2], ACT.Exp, bias=sk).then_inc(j_exp, 1)

        def scaled(j):
            act.wait_ge(j_rs, j + 1)
            c = 128 if j < HEADS else 192
            pj = p4[:, j % 4, :]
            nm = stmp[:, 8 * (j % 4):8 * (j % 4) + 8]
            A(pj[:, 0:c], pj[:, 0:c], ACT.Copy, scale=nm[:, 4:5])
            A(pj[:, c:384], pj[:, c:384], ACT.Copy, scale=nm[:, 5:6]).then_inc(j_p, 1)

        for t, ps in enumerate((bank[0], bank[1], pproj[:, 3, :])):
            r = P if t < 2 else NS
            act.wait_ge(t_ps, t + 1)
            A(knat[0:r, t, :], ps[0:r, 0:256], ACT.Copy)
            A(vnat[0:r, t, :], ps[0:r, 256:512], ACT.Copy).then_inc(t_sb, 1)
        act.wait_ge(s_cst, 48)
        exps(0)
        for j in range(20):
            scaled(j)
            if j + 1 < 20:
                exps(j + 1)
            act.wait_ge(j_pt, j + 1)
            if j >= 2:
                act.wait_ge(j_o, j - 1)
            pt, ps = pt2[:, j % 2, :], (bank[0], pproj[:, 2, :])[j % 2]
            if j < HEADS:
                A(pt[:, 0:384], ps[:, 0:384], ACT.Copy).then_inc(j_ptsb, 1)
            else:
                A(pt[:, 0:256], ps[:, 0:256], ACT.Copy)
                A(pt[0:NS, 256:512], ps[0:NS, 256:512], ACT.Copy).then_inc(j_ptsb, 1)
            if 4 <= j < 8:
                g = j - 4
                act.wait_ge(c_ps, g + 1)
                A(kct[:, 2 * g:2 * g + 2, :, :], pproj[:, 1, :].rearrange("p (b c s) -> p b c s", b=2, c=2), ACT.Copy)\
                    .then_inc(c_sb, 1)

        act.wait_ge(j_g, 20)
        act.wait_ge(kv_out, 16 * 18)

        def log_f(h):
            act.wait_ge(g_f, h + 1)
            A(fg[:], fg[:], ACT.Ln, scale=16.0).then_inc(g_ln, 1)

        def decays(h):
            act.wait_ge(g_d, h + 1)
            A(hbufs[h % 2][:], hbufs[h % 2][:], ACT.Exp).then_inc(g_e, 1)

        def rows_of_v(h):
            act.wait_ge(g_vt, h + 1)
            if h >= 1:
                act.wait_ge(g_vz, h)
            A(vn[:, 0:2, :], bank[3][:, 0:256].rearrange("p (t k) -> p t k", t=2), ACT.Copy)
            A(vn[0:NS, 2, :], bank[3][0:NS, 256:384], ACT.Copy).then_inc(g_vsb, 1)

        def rows_of_k(h):
            act.wait_ge(g_kt, h + 1)
            A(ken[:, 0:2, :], bank[3][:, 0:256].rearrange("p (t k) -> p t k", t=2), ACT.Copy)
            A(ken[0:NS, 2, :], bank[3][0:NS, 256:384], ACT.Copy).then_inc(g_ksb, 1)

        log_f(0)
        decays(0)
        rows_of_v(0)
        log_f(1)
        rows_of_k(0)
        for h in range(HH):
            if h + 1 < HH:
                decays(h + 1)
            act.wait_ge(g_o, 5 * h + 5)
            A(osb[:], pproj[:, 3, 0:T], ACT.Copy)
            A(osq[:], pproj[:, 3, 0:T], ACT.Square).then_inc(g_osq, 1)
            if h + 1 < HH:
                rows_of_v(h + 1)
            act.wait_ge(g_ms, h + 1)
            rsqrt(om[:, 1, :], om[:, 0, :]).then_inc(g_y, 1)
            if h + 1 < HH:
                rows_of_k(h + 1)
            if h + 2 < HH:
                log_f(h + 2)

        act.wait_ge(g_g, HH)
        act.wait_ge(hp_out, 16 * HH)
        act.wait_ge(hs_out, 16 * HH)
        for c in range(KC):
            A(hh[:, c, :], acts[:, C_Z + c, :], ACT.Copy).then_inc(h_hi, 1)

        def out0(i):
            for p in range(2):
                U = U_OUT0 + 2 * i + p

                def evac():
                    act.wait_ge(xc_new, 2 * i + p + 1)
                    A(hb, acts[:, ds(C_X1 + 4 * i + 2 * p, 2), :], ACT.Square).then_inc(h_sq, 1)
                around(U, evac)
        loop(act, 4, out0)
        token_rsqrt(1)
        with act.Fori(0, KC // 4) as i:
            for e in range(2):
                modulate(1, 2 * i + e, e)

        def in1(i):
            ada_evac(40 + i)
            for k in range(4):
                U = U_IN1 + 4 * i + k
                ps = pproj[:, 2 * (k % 2):2 * (k % 2) + 2, 0:T]

                def evac():
                    if k == 0:
                        act.wait_ge(bank_free[1], U_IN1 // 2 + 2 * i - 1)
                        A(u_sb, ps, ACT.Copy).then_inc(e_u, 1)
                    elif k == 3:
                        act.wait_ge(h_ready, 3 * KC + 2 * i)
                        A(sz, ps, ACT.Sigmoid).then_inc(e_z, 1)
                around(U, evac)
                if k == 3:
                    for m in range(2):
                        act.wait_ge(e_y, 2 * i + m + 1)
                        A(yh[:, ds(2 * i + m, 1), :], gc[:, m:m + 1, :], ACT.Copy).then_inc(e_yh, 1)
            act.wait_ge(e_cst, i + 1)
            act.wait_ge(stored, 32 * i + 16)
            A(csn[0:2], bank[2][0:2, 0:UC], ACT.Copy)
            A(csn[32:48], bank[3][0:16, 0:UC], ACT.Copy).then_inc(e_cso, 1)
        loop(act, 8, in1)
        def y_rows(u):
            act.wait_ge(f_t, u + 1)
            for t in range(3):
                r = P if t < 2 else NS
                last = A(ynat[0:r, t, ds(u * UC, UC)], bank[t][0:r, 0:UC], ACT.Copy)
            last.then_inc(f_e, 1)

        def out1(i):
            first, last = (isinstance(i, int) and i == n for n in (0, 3))
            for p in range(2):
                more = not (last and p == 1)
                for q in range(3 if more else 0):
                    split_hi(U_OUT1 + 2 * i + p + 1, q)
                if not (first and p == 0):
                    y_rows(2 * i + p - 1)
                if more:
                    split_hi(U_OUT1 + 2 * i + p + 1, 3)
        out1(0)
        with act.Fori(1, 3) as i:
            out1(i)
        out1(3)
        y_rows(7)

    @block.vector
    def _(dve):
        V = nc.vector
        st = Steps(dve, dve_s)
        tt, tsc, stt = V.tensor_tensor, V.tensor_scalar, V.scalar_tensor_tensor

        def split_lo(U, q):
            dve.wait_ge(hi_ready, 4 * U + q + 1)
            tt(wl[:, q], raw[:, q], wh[:, q].bitcast(F32), ALU.subtract).then_inc(lo_ready, 1)

        def around(U, evac, last=False):
            if not last:
                for q in range(3):
                    split_lo(U + 1, q)
            if evac:
                dve.wait_ge(quarter_used, 4 * U + 4)
                if not last:
                    dve.wait_ge(lo_ready, 4 * U + 7)
                evac()
            if not last:
                split_lo(U + 1, 3)

        def mod_out(G):
            dve.wait_ge(ada_sel, G + 1)
            tt(mods[:, ds(2 * G, 2), :], bank[1][:, 0:2 * NSEQ].rearrange("p (m s) -> p m s", m=2),
               adab[:, ds(2 * G, 2)][:, :, None].to_broadcast([P, 2, NSEQ]), ALU.add).then_inc(mod_done, 1)

        def seqs(ap):
            return ap.rearrange("p (b j) -> p b j", j=NJ)

        dve.wait_ge(csig, 1)
        dve.wait_ge(consts, 1)
        tt(cond[:, :, 0:NSEQ], bank[0][:, 0:KC * NSEQ].rearrange("p (c s) -> p c s", c=KC),
           soft[:, 0:KC * NSEQ].rearrange("p (c s) -> p c s", c=KC), ALU.mult).then_inc(cond_done, 1)
        dve.wait_ge(vecs_done, 1)
        st(tt(lb[:, 0, :], lbl, lbl, ALU.subtract))
        st.settle()
        V.memset(small[:, 27:28], 0.0).then_inc(lb_exp, 1)
        V.memset(ssq, 0.0).then_inc(sqr, 1)
        for c in range(KC):
            dve.wait_ge(h_sq, c + 1)
            dve.wait_ge(sqr, c + 1)
            tt(ssq, ssq, xsq[:, c % 2, :], ALU.add).then_inc(sqr, 1)
        dve.wait_ge(sqr, KC + 1)
        V.memset(small[:, 26:27], 0.0).then_inc(ss_done, 1)

        def newton(y, m, t):
            st(tt(t, y, y, ALU.mult))
            st.settle()
            st(stt(t, t, -0.5, m, ALU.mult, ALU.mult))
            st.settle()
            return stt(y, t, 1.5, y, ALU.add, ALU.mult)

        def token_norm(layer):
            dve.wait_ge(ss_sum, layer + 1)
            tsc(hb[:, 0, :], bank[2][:, 0:T], 1.0 / D, EPS, ALU.mult, ALU.add).then_inc(ms_ready, 1)
            dve.wait_ge(rs_ready, layer + 1)
            st(newton(rstd, hb[:, 0, :], hb[:, 1, :]))
            st.settle()

        def scales(layer, j, n):
            return st(stt(s1[:, ds(j, n), :], mods[:, ds(48 * layer + 16 + j, n), :], 1.0,
                          nw[:, ds(16 * layer + j, n)][:, :, None].to_broadcast([P, n, NSEQ]), ALU.add, ALU.mult))

        def modulate(layer, j, par, cx):
            n = KC // 2 * layer + j + 1
            h = hbs[par]
            tt(h, acts[:, ds(cx + 2 * j, 2), :], rstd[:, None, :].to_broadcast([P, 2, T]), ALU.mult).then_inc(h_nrm, 1)
            dve.wait_ge(h_nrm, n)
            hs = h[:, :, SEQ:T].rearrange("p c (b j) -> p c b j", j=NJ)
            s1c = s1[:, ds(2 * j, 2), 1:NSEQ][:, :, :, None].to_broadcast([P, 2, NB, NJ])
            sh = mods[:, ds(48 * layer + 2 * j, 2), 1:NSEQ][:, :, :, None].to_broadcast([P, 2, NB, NJ])
            st(tt(hs, hs, s1c, ALU.mult))
            st.settle()
            tt(hs, hs, sh, ALU.add).then_inc(hb_ready, 1)

        def low_part(layer, j, par):
            dve.wait_ge(h_hi, KC // 2 * layer + KC * layer + j + 1)
            tt(hl[:, ds(2 * j, 2), :], hbs[par], hh[:, ds(2 * j, 2), :].bitcast(F32), ALU.subtract).then_inc(h_ready, 2)

        token_norm(0)
        mod_out(0)
        mod_out(1)
        with dve.Fori(1, GA // 4) as i:
            mod_out(2 * i)
            mod_out(2 * i + 1)
        with dve.Fori(GA // 4, GA // 2) as i:
            st.enter(i - GA // 4, 4)
            for e in range(2):
                mod_out(2 * i + e)
                dve.wait_ge(mod_done, 2 * i + e + 1)
                scales(0, 2 * (2 * i + e - GA // 2), 2)
                st.settle()
                modulate(0, 2 * i + e - GA // 2, e, C_X0)
                low_part(0, 2 * i + e - GA // 2, e)
        st.leave(GA // 4)
        for q in range(4):
            split_lo(0, q)

        def head_norm(s, x, w):
            dve.wait_ge(n_sum, s + 1)
            for m in range(2):
                last = tsc(soft[:, m * T:m * T + T], bank[2 + m][:, 0:T], 1.0 / HD, EPS, ALU.mult, ALU.add)
            last.then_inc(n_ms, 1)
            dve.wait_ge(n_y, s + 1)
            y = soft[:, 2 * T:4 * T]
            st(newton(y, soft[:, 0:2 * T], norm[:, 2 * T:4 * T]))
            st.settle()
            stt(x, x, w, y.rearrange("p (m t) -> p m t", m=2), ALU.mult, ALU.mult).then_inc(n_q, 1)

        for name, U0, n, w, col, opset, G0 in phases:
            def body(i):
                for p in range(2):
                    U = U0 + 2 * i + p
                    evac = None
                    if name in ("za", "zb"):
                        def evac():
                            dve.wait_ge(z_sig, U - U_ZA + 1)
                            dve.wait_ge(stored, 16)
                            tt(acts[:, ds(C_Z + 2 * (U0 - U_ZA) + 4 * i + 2 * p, 2), :], pproj[:, 2 * p:2 * p + 2, 0:T],
                               hb, ALU.mult).then_inc(bank_free[p], 1)
                    if name == "qb":
                        def evac():
                            head_norm(2 * i + p + 1, acts[:, ds(C_Q + 4 * i + 2 * p, 2), :], qn)
                    around(U, evac)
                    if G0 is not None:
                        mod_out(G0 + 2 * i + p)
            loop(dve, n, body, *(((st, 6),) if name == "qb" else ()))
            if name == "q":
                head_norm(0, acts[:, C_K:C_K + 2, :], kn)

        dve.wait_ge(n_q, 5)
        V.tensor_copy(ksw[0:64], acts[64:128, C_K:C_K + 2, :])
        V.tensor_copy(ksw[64:128], acts[0:64, C_K:C_K + 2, :]).then_inc(k_sw, 1)

        def sample_queries():
            for kv in range(KVH):
                for half in range(2):
                    src, dst = slice(64 * half, 64 * half + 64), slice(64 * (kv % 2), 64 * (kv % 2) + 64)
                    for c in range(2):
                        last = V.tensor_copy(qs2[dst, kv // 2, :, 2 * c + half, :],
                                             seqs(acts[src, C_Q + 2 * kv + c, SEQ:T]))
            last.then_inc(q_st, 1)

        def smax(j):
            dve.wait_ge(j_sc, j + 1)
            if j >= 4:
                dve.wait_ge(j_pt, j - 3)
            pj = p4[:, j % 4, :]
            ps = (bank[2], bank[3], pproj[:, 0, :])[j % 3]
            nm = stmp[:, 8 * (j % 4):8 * (j % 4) + 8]
            c = 128 if j < HEADS else 192
            sk = sinkp[:, j:j + 1] if j < HEADS else sinks[:, 0:1]
            if j < HEADS:
                st(stt(pj, ps[:, 0:384], HD ** -0.5, pmask[:], ALU.mult, ALU.add))
            else:
                b = 2 * (j - HEADS)
                pv, psv = pj.rearrange("p (e k) -> p e k", e=2), ps[:, 0:384].rearrange("p (e k) -> p e k", e=2)
                st(stt(pv[:, :, 0:WIN], psv[:, :, 0:WIN], HD ** -0.5,
                       smask[:, 0:WIN][:, None, :].to_broadcast([P, 2, WIN]), ALU.mult, ALU.add))
                st(stt(pv[:, :, WIN:192], psv[:, :, WIN:192], HD ** -0.5,
                       smask[:, WIN + NS * b:WIN + NS * b + 2 * NS].rearrange("p (e k) -> p e k", e=2), ALU.mult, ALU.add))
            st.settle()
            V.reduce_max(nm[:, 6:7], pj[:, 0:c], AX.X)
            st(V.reduce_max(nm[:, 7:8], pj[:, c:384], AX.X))
            st.settle()
            tsc(nm[:, 0:2], nm[:, 6:8], sk, -1.0, ALU.max, ALU.mult).then_inc(j_max, 1)

        def denominators(j):
            dve.wait_ge(j_exp, j + 1)
            nm = stmp[:, 8 * (j % 4):8 * (j % 4) + 8]
            st(tt(nm[:, 2:4], nm[:, 2:4], nm[:, 4:6], ALU.add))
            st.settle()
            V.reciprocal(nm[:, 4:6], nm[:, 2:4]).then_inc(j_rs, 1)

        def gate_a(j):
            dve.wait_ge(j_o, j + 1)
            ps = (bank[1], pproj[:, 3, :])[j % 2]
            if j < HEADS:
                rows = slice(64 * (j % 2), 64 * (j % 2) + 64)
                z = acts[rows, C_Z + j // 2, 0:SEQ]
                tt(z, ps[rows, 0:SEQ], z, ALU.mult).then_inc(j_g, 1)
            else:
                for e in range(2):
                    b = 2 * (j - HEADS) + e
                    for r in range(2):
                        v = ps[0:64, P * e:P * e + P].rearrange("p (c r j) -> p c r j", r=2, j=NJ)[:, :, r, :]
                        z = acts[64 * r:64 * r + 64, C_Z:C_Z + 8, SEQ + NJ * b:SEQ + NJ * b + NJ]
                        last = tt(z, v, z, ALU.mult)
                last.then_inc(j_g, 1)

        dve.wait_ge(s_cst, 48)
        smax(0)
        smax(1)
        sample_queries()
        for j in range(20):
            denominators(j)
            if j + 2 < 20:
                smax(j + 2)
            if j >= 2:
                gate_a(j - 2)
        gate_a(18)
        gate_a(19)

        dve.wait_ge(kv_out, 16 * 18)
        dve.wait_ge(lb_exp, 2)
        st(V.reciprocal(lb[:, 2, :], lb[:, 1, :]))
        st.settle()
        st(tt(lb[:, 1, :], lb[:, 1, :], lb[:, 2, :], ALU.mult))
        st.settle()
        st(tt(lb[:, 2, :], lb[:, 1, :], lb[:, 1, :], ALU.subtract))
        st.settle()
        st(tsc(lb[:, 3, :], lb[:, 2, :], -1.0, 1.0, ALU.mult, ALU.add))
        st.settle()

        SPANS = ((0, SEQ, LEVELS), (NL * SEQ, NS, LEVELS[3:]))

        def forget(h):
            sg, kk = acts[:, C_S + h, :], acts[:, C_KB + h, :]
            lo, om1 = lb[:, 2, h:h + 1], lb[:, 3, h:h + 1]
            st(tsc(fg[:], sg, om1, lo, ALU.mult, ALU.add))
            st(tsc(kk, kk, om1, None, ALU.mult))
            st.settle()
            tsc(fg[:], fg[:], 1e-20, None, ALU.max).then_inc(g_f, 1)

        def exponents(h):
            dve.wait_ge(g_ln, h + 1)
            st(tsc(fg[:], fg[:], LN16, None, ALU.subtract))
            st.settle()
            hbuf = hbufs[h % 2]
            b, kd = hbuf[:, 1728:2048], hbuf[:, 2048:2368]
            st(V.tensor_tensor_scan(b, rmask[:], fg[:], 0.0, ALU.mult, ALU.add))
            st.settle()
            for n, (base, width, lv) in enumerate(SPANS):
                bt = b[:, 0:SEQ] if n == 0 else b[:, SEQ:T]
                for l, hf in enumerate(lv):
                    nb = width // (2 * hf)
                    bv = bt.rearrange("p (n e h) -> p n e h", e=2, h=hf)
                    wv = hbuf[:, base + l * width:base + (l + 1) * width].rearrange("p (n e h) -> p n e h", e=2, h=hf)
                    mid = bv[:, :, 0, hf - 1:hf].to_broadcast([P, nb, hf])
                    tt(wv[:, :, 0, :], mid, bv[:, :, 0, :], ALU.subtract)
                    tt(wv[:, :, 1, :], bv[:, :, 1, :], mid, ALU.subtract)
                c = 64 if n == 0 else NJ
                bv = bt.rearrange("p (n c) -> p n c", c=c)
                kv_ = (kd[:, 0:SEQ] if n == 0 else kd[:, SEQ:T]).rearrange("p (n c) -> p n c", c=c)
                last = tt(kv_, bv[:, :, c - 1:c].to_broadcast([P, width // c, c]), bv, ALU.subtract)
            last.then_inc(g_d, 1)

        def weighted(h):
            dve.wait_ge(g_e, h + 1)
            hbuf = hbufs[h % 2]
            b, kd = hbuf[:, 1728:2048], hbuf[:, 2048:2368]
            kk, qq = acts[:, C_KB + h, :], acts[:, C_QB + h, :]
            for n, (base, width, lv) in enumerate(SPANS):
                t = slice(0, SEQ) if n == 0 else slice(SEQ, T)
                for l, hf in enumerate(lv):
                    wv = hbuf[:, base + l * width:base + (l + 1) * width].rearrange("p (n e h) -> p n e h", e=2, h=hf)
                    kv_ = kk[:, t].rearrange("p (n e h) -> p n e h", e=2, h=hf)
                    qv = qq[:, t].rearrange("p (n e h) -> p n e h", e=2, h=hf)
                    tt(wv[:, :, 0, :], wv[:, :, 0, :], kv_[:, :, 0, :], ALU.mult)
                    tt(wv[:, :, 1, :], wv[:, :, 1, :], qv[:, :, 1, :], ALU.mult)
            tt(qebs[h % 2][:], b, qq, ALU.mult)
            tt(kd, kd, kk, ALU.mult).then_inc(g_w, 1)

        def masked(h):
            dve.wait_ge(g_sc, h + 1)
            for c in range(2):
                st(tt(sctmp[:, c, :], bank[c][:, 0:448], lmask[:].rearrange("p l t -> p (l t)"), ALU.mult))
            st(tt(sctmp[0:NS, 2, 0:256], bank[2][0:NS, 0:256], lmask[0:NS, 3:7, :].rearrange("p l t -> p (l t)"), ALU.mult))
            st.settle()
            for c in range(2):
                V.tensor_reduce(stt_[:, c, :], sctmp[:, c, :].rearrange("p (l t) -> p t l", l=NL + 1), AX.X, ALU.add)
            V.tensor_reduce(stt_[0:NS, 2, :], sctmp[0:NS, 2, 0:256].rearrange("p (l t) -> p t l", l=4), AX.X, ALU.add)\
                .then_inc(g_st, 1)

        def states(h):
            b = hbufs[h % 2][:, 1728:2048]
            dve.wait_ge(g_u, 3 * h + 2)
            if h >= 1:
                dve.wait_ge(hp_out, 16 * h)
            V.tensor_copy(sst[:, 0, :], pproj[:, 0, 0:P]).then_inc(g_s, 1)
            for c in range(1, 4):
                dve.wait_ge(g_s, 4 * h + c)
                stt(sst[:, c, :], sst[:, c - 1, :], b[:, 64 * c + 63:64 * c + 64], pproj[:, 0, c * P:c * P + P],
                    ALU.mult, ALU.add).then_inc(g_s, 1)

        def sample_states(h):
            b = hbufs[h % 2][:, 1728:2048]
            dve.wait_ge(g_o, 5 * h + 5)
            dve.wait_ge(g_u, 3 * h + 3)
            for n in range(NB):
                v = s0[:, h % 2, n, :]
                end = SEQ + NJ * n + NJ
                last = stt(v, v, b[:, end - 1:end], pproj[:, 1 + n // 4, (n % 4) * P:(n % 4) * P + P],
                           ALU.mult, ALU.add)
            last.then_inc(g_x, 1)

        def mean_square(h):
            dve.wait_ge(g_sum, h + 1)
            tsc(om[:, 0, :], pproj[:, 3, 0:T], 1.0 / DK, EPS, ALU.mult, ALU.add).then_inc(g_ms, 1)

        def gated(h):
            dve.wait_ge(g_y, h + 1)
            st(newton(om[:, 1, :], om[:, 0, :], osq[:]))
            st.settle()
            st(stt(osb[:], osb[:], hn, om[:, 1, :], ALU.mult, ALU.mult))
            st.settle()
            z = acts[:, C_Z + 8 + h, :]
            tt(z, z, osb[:], ALU.mult).then_inc(g_g, 1)

        forget(0)
        exponents(0)
        weighted(0)
        forget(1)
        for h in range(HH):
            masked(h)
            if h + 1 < HH:
                exponents(h + 1)
            states(h)
            if h + 1 < HH:
                weighted(h + 1)
            mean_square(h)
            sample_states(h)
            if h + 2 < HH:
                forget(h + 2)
            gated(h)

        dve.wait_ge(hp_out, 16 * HH)
        dve.wait_ge(hs_out, 16 * HH)
        for c in range(KC):
            dve.wait_ge(h_hi, KC // 2 + c + 1)
            tt(hl[:, c, :], acts[:, C_Z + c, :], hh[:, c, :].bitcast(F32), ALU.subtract).then_inc(h_ready, 1)

        def residual(i, p, gate, out_sem, out):
            for m in range(2):
                c = 4 * i + 2 * p + m
                g = mods[:, ds(gate + c, 1), :].rearrange("p c s -> p (c s)")
                x = acts[:, ds(C_X1 + c, 1), 0:SEQ].rearrange("p c t -> p (c t)")
                y = out[:, m:m + 1, 0:SEQ].rearrange("p c t -> p (c t)")
                ps = pproj[:, 2 * p + m, 0:T]
                st(tt(seqs(gtmp[:, m, :]), seqs(ps[:, SEQ:T]), g[:, 1:NSEQ][:, :, None].to_broadcast([P, NB, NJ]), ALU.mult))
                last = stt(y, ps[:, 0:SEQ], g[:, 0:1], x, ALU.mult, ALU.add)
            last.then_inc(bank_free[p], 1)
            st.settle()
            tt(out[:, :, SEQ:T], acts[:, ds(C_X1 + 4 * i + 2 * p, 2), SEQ:T], gtmp, ALU.add).then_inc(out_sem, 1)

        dve.wait_ge(x1_loaded, 16)
        st(V.memset(ssq, 0.0))

        def out0(i):
            for p in range(2):
                def evac():
                    residual(i, p, 32, xc_new, acts[:, ds(C_X1 + 4 * i + 2 * p, 2), :])
                    dve.wait_ge(h_sq, KC + 2 * i + p + 1)
                    for m in range(2):
                        st(tt(ssq, ssq, hb[:, m, :], ALU.add))
                        st.settle()
                around(U_OUT0 + 2 * i + p, evac)
        loop(dve, 4, out0, (st, 8))
        V.memset(small[:, 26:27], 0.0).then_inc(ss_done, 1)
        scales(1, 0, KC)
        token_norm(1)
        with dve.Fori(0, KC // 4) as i:
            st.enter(i, 2)
            dve.wait_ge(h_ready, 2 * KC + 4 * i)
            for e in range(2):
                modulate(1, 2 * i + e, e, C_X1)
            for e in range(2):
                low_part(1, 2 * i + e, e)
        st.leave(KC // 4)

        st(V.memset(cin[:, :, 0:2], 0.0))

        def in1(i):
            for k in range(4):
                U = U_IN1 + 4 * i + k
                ps = pproj[:, 2 * (k % 2):2 * (k % 2) + 2, 0:T]

                def evac():
                    if k == 0:
                        dve.wait_ge(e_u, i + 1)
                        V.memset(small[:, 28:29], 0.0).then_inc(bank_free[0], 1)
                        for m in range(2):
                            V.tensor_copy(cin[:, m, 258:338].rearrange("p (b c) -> p b c", c=10)[:, :, 0:2],
                                          sct[:, ds(2 * i + m, 1), :].rearrange("p c (b r) -> p (c b) r", r=2))
                    elif k == 1:
                        tt(cin[:, :, 2:258], ps[:, :, 0:SEQ], u_sb[:, :, 0:SEQ], ALU.mult)
                        for m in range(2):
                            cs = cin[:, m, 258:338].rearrange("p (b c) -> p b c", c=10)
                            last = tt(cs[:, :, 2:10], seqs(ps[:, m, SEQ:T]), seqs(u_sb[:, m, SEQ:T]), ALU.mult)
                        st(last)
                        st.settle()
                        V.memset(small[:, 28:29], 0.0).then_inc(bank_free[1], 1)
                        for m in range(2):
                            cs = cin[:, m, 258:338].rearrange("p (b c) -> p b c", c=10)
                            cl = cst[:, m, :]
                            V.tensor_copy(cl[:, 0:2], cin[:, m, 256:258])
                            V.tensor_copy(cl[:, 2:18].rearrange("p (b r) -> p b r", r=2), cs[:, :, 8:10]).then_inc(e_cs, 1)
                        for tap in range(3):
                            for m in range(2):
                                w = cw[:, tap, ds(2 * i + m, 1)]
                                x = cin[:, m, tap:tap + 336]
                                if tap == 0:
                                    st(tsc(cv[:, m, :], x, w, None, ALU.mult))
                                else:
                                    st(stt(cv[:, m, :], x, w, cv[:, m, :], ALU.mult, ALU.add))
                            st.settle()
                    elif k == 2:
                        for m in range(2):
                            tt(gc[:, m, 0:SEQ], ps[:, m, 0:SEQ], cv[:, m, 0:SEQ], ALU.mult)
                            cs = cv[:, m, 256:336].rearrange("p (b c) -> p b c", c=10)
                            last = tt(seqs(gc[:, m, SEQ:T]), seqs(ps[:, m, SEQ:T]), cs[:, :, 2:10], ALU.mult)
                        st(last)
                        st.settle()
                        V.memset(small[:, 28:29], 0.0).then_inc(bank_free[0], 1)
                    else:
                        dve.wait_ge(e_z, i + 1)
                        st(tt(sz, sz, ps, ALU.mult))
                        st.settle()
                        V.memset(small[:, 28:29], 0.0).then_inc(bank_free[1], 1)
                        for m in range(2):
                            tt(gc[:, m, :], gc[:, m, :], sz[:, m, :], ALU.mult).then_inc(e_y, 1)
                around(U, evac)
                if k == 3:
                    for m in range(2):
                        dve.wait_ge(e_yh, 2 * i + m + 1)
                        tt(yl[:, ds(2 * i + m, 1), :], gc[:, m:m + 1, :], yh[:, ds(2 * i + m, 1), :].bitcast(F32),
                           ALU.subtract).then_inc(h_ready, 1)
            mod_out(40 + i)
        loop(dve, 8, in1, (st, 9))

        def out1(i):
            for p in range(2):
                around(U_OUT1 + 2 * i + p, lambda: residual(i, p, 80, f_x, xo[p]))
        loop(dve, 3, out1, (st, 4))
        around(U_END - 2, lambda: residual(3, 0, 80, f_x, xo[0]))
        around(U_END - 1, lambda: residual(3, 1, 80, f_x, xo[1]), True)

    ctx.close()


_INS = ["x_prompt", "x_sample", "cache_k", "cache_v", "state_hgrn", "state_conv", "c_prompt", "c_sample", "norm_w",
        "ada_w", "ada_b", "even_w_in", "even_w_out", "q_norm_w", "k_norm_w", "attn_sinks", "hgrn_lb_logits",
        "hgrn_norm_w", "odd_w_in", "odd_conv_w", "odd_w_out"]
_OUTS = [("y_p", (1, SEQ, D)), ("y_s", (NB, NJ, D)), ("ck_p", (1, 1, WIN, KVH, HD)), ("cv_p", (1, 1, WIN, KVH, HD)),
         ("sh_p", (1, 1, HH, DK, DK)), ("sc_p", (1, 1, 2, D)), ("ck_s", (1, NB, WIN, KVH, HD)),
         ("cv_s", (1, NB, WIN, KVH, HD)), ("sh_s", (1, NB, HH, DK, DK)), ("sc_s", (1, NB, 2, D))]


def kernel(**inputs):
    import numpy as _np
    import concourse.bacc as _bacc
    from concourse import mybir as _mybir
    from concourse.bass_utils import run_bass_kernel_spmd as _run

    nc = _bacc.Bacc("TRN2", target_bir_lowering=False, num_devices=1)
    arrays, a, o = {}, {}, {}
    for name in _INS:
        arrays[f"in_{name}"] = x = _np.ascontiguousarray(inputs[name])
        a[name] = nc.dram_tensor(f"in_{name}", x.shape, _mybir.dt.from_np(x.dtype), kind="ExternalInput").ap()
    for name, shape in _OUTS:
        o[name] = nc.dram_tensor(f"out_{name}", shape, _mybir.dt.float32, kind="ExternalOutput").ap()
    hybrid_step_kernel(nc, a, o)
    r = _run(nc, [arrays], core_ids=[0])
    return tuple(r.results[0][f"out_{name}"] for name, _ in _OUTS)
```

```python
from contextlib import ExitStack

import concourse.bass as bass
from concourse import mybir

F32 = mybir.dt.float32
F32R = mybir.dt.float32r
ALU = mybir.AluOpType
ACT = mybir.ActivationFunctionType
AX = mybir.AxisListType
ds = bass.ds

P = 128
D = 2048
KC = D // P
SEQ, NB, NJ = 256, 8, 8
NS = NB * NJ
T = SEQ + NS
NSEQ = 1 + NB
UC = 256
QK = 4
HEADS, KVH, HD, WIN = 16, 4, 64, 128
HH, DK = 8, 128
EPS = 1e-6
LN16 = 2.772588722239781
LEVELS = [32, 16, 8, 4, 2, 1]
NL = len(LEVELS)

U_KV, U_Q, U_QB, U_F, U_I, U_ZA, U_ZB, U_OUT0, U_IN1, U_OUT1 = 0, 2, 6, 10, 14, 18, 22, 26, 34, 66
U_END = 74
C_Q, C_K, C_V, C_QB, C_S, C_KB, C_I, C_Z = 0, 8, 10, 12, 20, 28, 36, 44
C_END = 60
C_X0 = C_Z
C_X1 = 0
C_Y = 20
C_IN = 0
GA = 16


class Steps:

    def __init__(self, eng, sem):
        self.eng, self.sem, self.n, self.reg, self.per = eng, sem, 0, None, 0

    def __call__(self, ins):
        ins.then_inc(self.sem, 1)
        self.n += 1
        return ins

    def settle(self):
        self.eng.wait_ge(self.sem, self.n if self.reg is None else self.reg * self.per + self.n)

    def enter(self, reg, per):
        self.reg, self.per, self.start = reg, per, self.n

    def leave(self, times):
        assert self.n - self.start == self.per, (self.n - self.start, self.per)
        self.n = self.start + self.per * times
        self.reg = None


def hybrid_step_kernel(nc, a, o):
    ctx = ExitStack()

    def sem(name):
        return ctx.enter_context(nc.semaphore(name))

    at = [16512]

    def sb(name, shape, dt=F32, where=None):
        size = 4
        for n in shape[1:]:
            size *= n
        size = (size + 31) // 32 * 32
        if where is None:
            where = at[0]
            at[0] += size
        return nc.alloc_sbuf_tensor_at(name, shape, dt, offset=where)

    raw = sb("raw", [P, 4, QK, UC])
    wh = sb("wh", [P, 4, QK, UC], F32R)
    o_wl = at[0]
    wl = sb("wl", [P, 4, QK, UC], F32R)
    adaw2 = sb("adaw2", [P, 4, QK, UC], F32, o_wl)
    o_adaw = at[0]
    adaw = sb("adaw", [P, 4, QK, UC])
    o_h = at[0]
    hh = sb("hh", [P, KC, T], F32R)
    hl = sb("hl", [P, KC, T], F32R)
    o_acts = at[0]
    acts = sb("acts", [P, C_END, T])
    yh = sb("yh", [P, KC, T], F32R, o_acts + C_Y * T * 4)
    yl = sb("yl", [P, KC, T], F32R, o_acts + (C_Y + KC) * T * 4)
    ident = sb("ident", [P, P])
    ones = sb("ones", [P, P])
    blk = sb("blk", [P, P])
    sel = sb("sel", [P, NSEQ])
    place = sb("place", [P, 32])
    seqm = sb("seqm", [NS, NB // 2])
    rmask = sb("rmask", [P, T])
    lmask = sb("lmask", [P, NL + 1, 64])
    pmask = sb("pmask", [P, 384])
    smask = sb("smask", [P, WIN + NB * NS])
    rep8 = sb("rep8", [NJ, P])
    cond = sb("cond", [P, KC, 32])
    mods = sb("mods", [P, 96, NSEQ])
    vecs = sb("vecs", [P, 96 + 92])
    s1 = sb("s1", [P, KC, NSEQ])
    adas = sb("adas", [P, UC])
    sct = sb("sct", [P, KC, 2 * NB])
    sinkp = sb("sinkp", [P, HEADS])
    sinks = sb("sinks", [P, 1])
    lb = sb("lb", [P, 4, HH])
    stmp = sb("stmp", [P, 2 * NS])
    norm = sb("norm", [P, 1280])
    soft = sb("soft", [P, 1280])
    assert at[0] <= nc.sbuf_usable_end, at[0]

    ssq, rstd, hb = norm[:, 0:T], norm[:, T:2 * T], norm[:, 2 * T:4 * T].rearrange("p (a t) -> p a t", a=2)
    hbs = [hb, soft[:, 2 * T:4 * T].rearrange("p (a t) -> p a t", a=2)]
    adab = vecs[:, 0:96]
    V2 = 96
    nw = vecs[:, V2:V2 + 32]
    cw = vecs[:, V2 + 32:V2 + 80].rearrange("p (i c) -> p i c", i=3)
    lbl = vecs[:, V2 + 80:V2 + 88]
    qn, kn, hn = (vecs[:, V2 + 88 + n:V2 + 89 + n] for n in range(3))

    def cols(c0, n, w, rows=P):
        return acts[0:rows, c0:c0 + (n * w + T - 1) // T, :].rearrange("p c t -> p (c t)")[:, 0:n * w].rearrange(
            "p (n w) -> p n w", n=n)

    xnat = cols(0, 3, D)
    cnat = cols(20, 1, D, NSEQ)
    scnat = cols(28, 1, D, 2 * NB)
    vnat1 = cols(36, 1, P, 96)
    vnat2 = cols(37, 1, P, 91)
    m8 = cols(38, 1, WIN + NB * 72, NJ)
    xsq = cols(41, 2, T)

    def scratch(name, shape, off):
        return sb(name, shape, F32, o_h + 4 * off)

    PW = 386
    p4 = sb("p4", [P, 4, PW], F32, o_adaw)
    qs2 = sb("qs2", [P, 2, NB, 4, NJ], F32, o_adaw + 4 * 4 * 388)
    knat = scratch("knat", [P, 3, 256], 2560)
    vnat = scratch("vnat", [P, 3, 256], 3328)
    vc = scratch("vc", [P, NB, 256], 4096)
    kct = scratch("kct", [P, NB, 2, P], 6144)
    ckn = scratch("ckn", [P, NB, 256], 8192)
    pt2 = soft[:, 0:1024].rearrange("p (a k) -> p a k", a=2)
    ksw = norm[:, 0:2 * T].rearrange("p (c t) -> p c t", c=2)
    O_KD = NL * SEQ + 3 * NS
    O_B = O_KD + T
    HB = O_B + T
    hbufs = [scratch("hbuf0", [P, HB], 0), sb("hbuf1", [P, HB], F32, o_acts)]
    qebs = [sb("qeb0", [P, T], F32, o_adaw + 4 * (3 * NB * P + 4 * P)), sb("qeb1", [P, T], F32, o_acts + 4 * HB)]
    vns = scratch("vn", [P, 2, 3, P], 2688)
    ken = scratch("ken", [P, 3, P], 3456)
    sctmp = scratch("sctmp", [P, 3, 448], 3840)
    stts = scratch("stt", [P, 2, 3, 64], 8192)
    s0 = sb("s0", [P, 3, NB, P], F32, o_adaw)
    sst = sb("sst", [P, 4, P], F32, o_adaw + 4 * 3 * NB * P)
    vz = scratch("vz", [NS, NB // 2, P], KC * T + HH * T)
    osb = scratch("osb", [P, T], 8704)
    osq = scratch("osq", [P, T], 9024)
    om = scratch("om", [P, 2, T], 9344)
    onat = scratch("onat", [P, 2, P], 9984)
    orow = hbufs[1][:, 0:2 * T]

    xspill = nc.dram_tensor("xspill", [P, KC * T], F32, kind="Internal").ap()

    bank = [ctx.enter_context(nc.psum_tensor(f"bank{n}", [P, 512], F32)) for n in range(4)]
    pproj = ctx.enter_context(nc.psum_tensor("pproj", [P, 4, 512], F32))

    s_wq = [sem(f"w_landed{n}") for n in range(4)]
    s_aq = [sem(f"ada_landed{n}") for n in range(4)]
    s_aq2 = [sem(f"ada2_landed{n}") for n in range(4)]
    h_nrm, h_aff = sem("h_normed"), sem("h_affine")
    s_cst, s_vec, s_xin, s_cin, s_scin = (sem(x) for x in ("const_landed", "vec_landed", "x_landed", "c_landed", "sc_landed"))
    hi_ready, lo_ready, quarter_used = (sem(x) for x in ("hi_ready", "lo_ready", "quarter_used"))
    h_sq, xc_new, lb_exp = sem("squared"), sem("x1_written"), sem("lb_exp")
    hp_out = sem("prompt_state_stored")
    bank_free = [sem("bank_free0"), sem("bank_free1")]
    h_hi, h_ready, hb_ready = sem("h_hi"), sem("h_ready"), sem("hb_ready")
    ada_used, ada_out, ada_sel, mod_done = (sem(x) for x in ("ada_used", "ada_out", "ada_sel", "mod_done"))
    pool_s, dve_s, act_s = sem("pool_steps"), sem("dve_steps"), sem("act_steps")
    consts = sem("consts")
    s_tp, s_tpe = sem("start_transposed"), sem("start_evacuated")
    vecs_done = sem("vecs_done")
    csig, cond_done = sem("csig"), sem("cond_done")
    stored, x1_loaded = sem("x_and_conv_state_stored"), sem("x_reloaded")
    ss_done, ss_sum, ms_ready, rs_ready = sem("ss_done"), sem("ss_summed"), sem("ms_ready"), sem("rs_ready")
    sqr = sem("sq_ready")
    xc_act = sem("xt_written")
    z_sig = sem("z_sigmoid")
    cache_in, kv_out = sem("caches_landed"), sem("kv_stored")
    n_sq, n_sum, n_ms, n_y, n_q = (sem(x) for x in ("qk_squared", "qk_summed", "qk_mean", "qk_rsqrt", "qk_normed"))
    t_ps, t_sb, k_sw, j_rs = sem("kv_transposed"), sem("kv_evacuated"), sem("k_exchanged"), sem("job_scale")
    q_st, c_ps, c_sb = sem("sample_queries"), sem("cached_k_transposed"), sem("cached_k_ready")
    j_sc, j_max, j_exp, j_p, j_pt, j_ptsb, j_o, j_g = (
        sem(x) for x in ("job_scores", "job_max", "job_exp", "job_probs", "job_pT", "job_pT_sb", "job_out", "job_gated"))
    g_f, g_ln, g_d, g_e, g_w, g_vt, g_vsb, g_kt, g_ksb = (
        sem(x) for x in ("hg_f", "hg_ln", "hg_diff", "hg_exp", "hg_weighted", "hg_vT", "hg_v", "hg_kT", "hg_k"))
    g_sc, g_st, g_u, g_s, g_o, g_osq, g_sum, g_ms, g_y, g_g, g_x = (
        sem(x) for x in ("hg_scores", "hg_masked", "hg_update", "hg_state", "hg_out", "hg_outsq", "hg_sum", "hg_mean",
                         "hg_rsqrt", "hg_gated", "hg_samples"))
    g_on, g_onsb = sem("hg_sample_rows"), sem("hg_sample_rows_sb")
    g_sd, g_nt = sem("hg_decayed"), sem("hg_rownorm")
    rsel, g_xb, g_rt = sem("row_select"), sem("hg_root_spread"), sem("hg_roots")
    s0_in, hs_out, g_vz = [sem(f"s0_landed{n}") for n in range(3)], sem("state_stored"), sem("hg_vz")
    e_cs, e_cst, e_cso = sem("cin_ready"), sem("cs_transposed"), sem("cs_evac")
    e_z, e_y, e_yh = sem("z1_sigmoid"), sem("y_f32"), sem("y_hi")
    f_x, f_t, f_e, y_out = sem("x2_ready"), sem("x2_transposed"), sem("y_evac"), sem("y_stored")
    passthru = sem("cache_copied")

    def wview(w):
        return w.rearrange("(k p) n -> p k n", p=P)

    w_in0, w_out0 = wview(a["even_w_in"][0]), wview(a["even_w_out"][0])
    w_in1, w_out1 = wview(a["odd_w_in"][0]), wview(a["odd_w_out"][0])
    w_ada = [wview(a["ada_w"][n]) for n in range(2)]

    B = UC
    phases = [
        ("kv", U_KV, 1, w_in0, lambda i: 4 * B, 0, None),
        ("q", U_Q, 2, w_in0, lambda i: 2 * i * B, 0, 16),
        ("qb", U_QB, 2, w_in0, lambda i: 10 * B + 2 * i * B, 0, 20),
        ("f", U_F, 2, w_in0, lambda i: 14 * B + 2 * i * B, 0, 24),
        ("i", U_I, 2, w_in0, lambda i: 18 * B + 2 * i * B, 0, 28),
        ("za", U_ZA, 2, w_in0, lambda i: 6 * B + 2 * i * B, 0, 32),
        ("zb", U_ZB, 2, w_in0, lambda i: 22 * B + 2 * i * B, 0, 36),
    ]

    def loop(eng, n, body, *steps):
        if n == 1:
            body(0)
            return
        with eng.Fori(0, n) as i:
            for s, per in steps:
                s.enter(i, per)
            body(i)
        for s, _ in steps:
            s.leave(n)

    ynat = scratch("ynat", [P, 3, D], 0)
    csn = soft[0:48, 0:UC]

    cst = sb("cst", [P, 2, 18], F32, o_acts + 52 * T * 4)
    u_sb = acts[:, 53:55, :]
    gc = acts[:, 55:57, :]
    sz = acts[:, 57:59, :]
    cin = acts[:, 16:20, :].rearrange("p c t -> p (c t)")[:, 0:2 * 338].rearrange("p (m t) -> p m t", m=2)
    cv = norm[:, 0:2 * 336].rearrange("p (m t) -> p m t", m=2)
    xo = [acts[:, 16:18, :], acts[:, 18:20, :]]
    gtmp = stmp[:, :].rearrange("p (m t) -> p m t", m=2)

    def hgrn_store(pool, h):
        pool.wait_ge(g_s, 4 * h + 4)
        pool.dma_start(o["sh_p"][0, 0, h], sst[:, 3]).then_inc(hp_out, 16)
        pool.wait_ge(g_x, h + 1)
        pool.dma_start(o["sh_s"][0, :, h].rearrange("b k v -> k b v"), s0[:, h % 3]).then_inc(hs_out, 16)

    block = ctx.enter_context(nc.Block())

    @block.sync
    def _(sp):
        sp.dma_start(cnat[0:1, 0, :], a["c_prompt"]).then_inc(s_cin, 16)
        sp.dma_start(cnat[1:NSEQ, 0, :], a["c_sample"]).then_inc(s_cin, 16)
        sp.dma_start(vnat1[:, 0, :], a["ada_b"].rearrange("l (c p) -> (l c) p", p=P)).then_inc(s_vec, 16)
        sp.dma_start(vnat2[0:32, 0, :], a["norm_w"].rearrange("l (c p) -> (l c) p", p=P)).then_inc(s_vec, 16)
        sp.dma_start(vnat2[32:80, 0, :], a["odd_conv_w"].rearrange("l i (c p) -> (l i c) p", p=P)).then_inc(s_vec, 16)
        sp.dma_start(vnat2[80:88, 0, :], a["hgrn_lb_logits"].rearrange("l (c p) -> (l c) p", p=P)).then_inc(s_vec, 16)
        for n, name in ((0, "q_norm_w"), (1, "k_norm_w")):
            for half in range(2):
                sp.dma_start(vnat2[88 + n:89 + n, 0, 64 * half:64 * half + 64], a[name]).then_inc(s_vec, 16)
        sp.dma_start(vnat2[90:91, 0, :], a["hgrn_norm_w"]).then_inc(s_vec, 16)
        sp.dma_start(scnat[:, 0, :], a["state_conv"].rearrange("l b r d -> (l b r) d")).then_inc(s_scin, 16)

        def load_ada(G, col, layer):
            for s in range(4):
                sp.wait_ge(ada_used, 4 * G - 3 + s)
                sp.dma_start(adaw[:, s], w_ada[layer][:, QK * s:QK * s + QK, ds(col, UC)]).then_inc(s_aq[s], 16)

        def load_ada_pair(i):
            for e, (buf, landed) in enumerate(((adaw, s_aq), (adaw2, s_aq2))):
                for s in range(4):
                    if not (isinstance(i, int) and i == 0):
                        sp.wait_ge(ada_used, 8 * i + 4 * e - 7 + s)
                    sp.dma_start(buf[:, s], w_ada[0][:, QK * s:QK * s + QK, ds((2 * i + e) * UC, UC)])\
                        .then_inc(landed[s], 16)

        def load_unit(U, w, col, wait=True):
            for q in range(4):
                if wait:
                    sp.wait_ge(lo_ready, 4 * U + q - 3)
                sp.dma_start(raw[:, q], w[:, QK * q:QK * q + QK, ds(col, UC)]).then_inc(s_wq[q], 16)

        load_ada_pair(0)
        for t in range(2):
            sp.dma_start(xnat[:, t, :], a["x_prompt"][0, t * P:(t + 1) * P, :]).then_inc(s_xin, 16)
        sp.dma_start(xnat[0:NS, 2, :], a["x_sample"].rearrange("b j d -> (b j) d")).then_inc(s_xin, 16)
        with sp.Fori(1, GA // 2) as i:
            load_ada_pair(i)
        for name, U0, n, w, col, _, G0 in phases:
            def body(i):
                for p in range(2):
                    U = U0 + 2 * i + p
                    if G0 is not None:
                        g = G0 if G0 < 24 else G0 - 24
                        load_ada(G0 + 2 * i + p, (g + 2 * i + p) * UC, G0 // 24)
                    load_unit(U, w, col(i) + p * UC, name != "kv" or p > 0)
            loop(sp, n, body)

        def out0(i):
            for p in range(2):
                load_unit(U_OUT0 + 2 * i + p, w_out0, (2 * i + p) * UC)
        loop(sp, 4, out0)

        def in1(i):
            load_ada(40 + i, (16 + i) * UC, 1)
            for k, part in enumerate((0, 1, 2, 3)):
                load_unit(U_IN1 + 4 * i + k, w_in1, part * D + i * UC)
        loop(sp, 8, in1)

        def out1(i):
            for p in range(2):
                load_unit(U_OUT1 + 2 * i + p, w_out1, (2 * i + p) * UC)
        loop(sp, 4, out1)

    @block.gpsimd
    def _(pool):
        g = nc.gpsimd
        steps = Steps(pool, pool_s)

        def st(ins):
            steps(ins)
            steps.settle()

        def select(out, pattern, base, mult, op, fill):
            st(g.affine_select(out=out, in_=out, compare_op=op, fill=fill, base=base, pattern=pattern,
                               channel_multiplier=mult))

        st(g.memset(ident[:], 0.0))
        select(ident[:], [[-1, P]], 0, 1, ALU.not_equal, 1.0)
        st(g.memset(cond[:], 0.0))
        st(g.memset(sel[:], 0.0))
        for j in range(4):
            select(sel[:], [[-1, NSEQ]], -32 * j, 1, ALU.not_equal, 1.0)
        g.memset(ones[:], 1.0).then_inc(consts, 1)
        pool.wait_ge(consts, 1)
        st(g.memset(blk[:], 0.0))
        st(g.memset(seqm[:], 1.0))
        st(g.memset(rmask[:], 1.0))
        st(g.memset(lmask[:], 0.0))
        st(g.memset(pmask[:], 0.0))
        st(g.memset(m8[:, 0, :], -1e30))
        st(g.memset(rep8[:], 0.0))
        m8v = m8[:, 0, :]
        st(g.memset(m8v[:, 0:WIN], 0.0))
        st(g.memset(m8v[:, WIN:].rearrange("p (n c) -> p n c", c=72)[:, :, 0:NJ], 0.0))
        select(m8v[:, 0:WIN], [[1, WIN]], 0, -1, ALU.is_ge, -1e30)
        select(m8v[:, WIN:].rearrange("p (n c) -> p n c", c=72)[:, :, 0:NJ], [[0, NB], [-1, NJ]], 0, 1, ALU.is_ge, -1e30)
        select(rep8[:].rearrange("p (n j) -> p n j", j=NJ), [[0, 16], [-1, NJ]], 0, 1, ALU.not_equal, 1.0)
        st(g.memset(blk[0:64, 0:64], 1.0))
        g.memset(blk[64:128, 64:128], 1.0).then_inc(consts, 1)
        pool.wait_ge(consts, 2)
        st(g.memset(rmask[:, 0:SEQ].rearrange("p (n c) -> p n c", c=64)[:, :, 0:1], 0.0))
        st(g.memset(rmask[:, SEQ:T].rearrange("p (n c) -> p n c", c=NJ)[:, :, 0:1], 0.0))
        st(g.memset(place[:], 0.0))
        select(place[:].rearrange("p (g j) -> p g j", j=NJ), [[-40, 4], [-1, NJ]], 0, 1, ALU.not_equal, 1.0)
        for l, h in enumerate(LEVELS):
            st(g.memset(lmask[0:64, l, :].rearrange("p (n e h) -> p n e h", e=2, h=h)[:, :, 1, :], 1.0))
        for e in range(2):
            v = seqm[32 * e:32 * e + 32, :]
            select(v, [[-NJ, NB // 2]], 0, 1, ALU.is_ge, 0.0)
            select(v, [[NJ, NB // 2]], NJ - 1, -1, ALU.is_ge, 0.0)
        for l, h in enumerate(LEVELS):
            v = lmask[0:64, l, :].rearrange("p (n e h) -> p n e h", e=2, h=h)
            n = 64 // (2 * h)
            select(v, [[-2 * h, n], [0, 2], [0, h]], 0, 1, ALU.is_ge, 0.0)
            select(v, [[2 * h, n], [0, 2], [0, h]], h - 1, -1, ALU.is_ge, 0.0)
        select(lmask[0:64, NL, :], [[-1, 64]], 0, 1, ALU.not_equal, 1.0)
        select(pmask[:, 0:128], [[-1, 128]], 0, 1, ALU.is_ge, -1e30)
        select(pmask[:, 128:384], [[1, 256]], 0, -1, ALU.is_ge, -1e30)
        select(pmask[:, 128:384], [[-1, 256]], WIN, 1, ALU.is_ge, -1e30)
        pool.dma_start(lmask[64:128], lmask[0:64]).then_inc(s_cst, 16)
        pool.dma_start(sinkp[:, :], a["attn_sinks"][0:1, :].partition_broadcast(P)).then_inc(s_cst, 16)
        with nc.allow_non_contiguous_dma("128 sink values, once"):
            pool.dma_start(sinks[:, :], a["attn_sinks"][0, :][:, None].to_broadcast([HEADS, NJ])).then_inc(s_cst, 16)
        pool.wait_ge(xc_act, KC)
        pool.wait_ge(quarter_used, 8)
        pool.dma_start(xspill, acts[:, C_X0:C_X0 + KC, :].rearrange("p c t -> p (c t)")).then_inc(stored, 16)
        pool.wait_ge(quarter_used, 4 * U_OUT0)
        pool.dma_start(ckn[:], a["cache_k"][0].rearrange("b s k d -> s b (k d)")).then_inc(cache_in, 16)
        pool.dma_start(vc[:], a["cache_v"][0].rearrange("b s k d -> s b (k d)")).then_inc(cache_in, 16)
        for n, (src, dst) in enumerate((("cache_k", "ck_s"), ("cache_v", "cv_s"))):
            pool.dma_start(o[dst][0, :, 0:WIN - NJ].rearrange("b s k d -> b (s k d)"),
                           a[src][0, :, NJ:WIN].rearrange("b s k d -> b (s k d)")).then_inc(passthru, 16)
        pool.wait_ge(t_sb, 3)
        for n, (src, dp, dst) in enumerate(((knat, "ck_p", "ck_s"), (vnat, "cv_p", "cv_s"))):
            pool.dma_start(o[dp][0, 0].rearrange("s k d -> s (k d)"), src[:, 1, :]).then_inc(kv_out, 16)
            for b in range(NB):
                pool.dma_start(o[dst][0, b, WIN - NJ:WIN].rearrange("s k d -> s (k d)"),
                               src[NJ * b:NJ * b + NJ, 2, :]).then_inc(kv_out, 16)
        pool.wait_ge(n_q, 5)
        st(g.memset(blk[:], 0.0))
        for k in range(3):
            select(blk[:], [[0, P]], -32 * k, 1, ALU.not_equal, 1.0)
        g.affine_select(out=blk[:], in_=blk[:], compare_op=ALU.not_equal, fill=1.0, base=-96, pattern=[[0, P]],
                        channel_multiplier=1).then_inc(rsel, 1)
        pool.wait_ge(rsel, 1)
        pool.wait_ge(j_g, 20)
        pool.wait_ge(kv_out, 16 * 18)
        def load_states(h):
            if h >= 3:
                pool.wait_ge(hs_out, 16 * (h - 2))
            pool.dma_start(s0[:, h % 3], a["state_hgrn"][0, :, h].rearrange("b k v -> k b v")).then_inc(s0_in[h % 3], 16)

        for h in range(3):
            load_states(h)
        for h in range(HH):
            pool.wait_ge(g_vsb, h + 1)
            if h >= 1:
                pool.wait_ge(g_u, 3 * h)
            g.tensor_tensor(vz[:], vns[0:NS, h % 2, 2, :][:, None, :].to_broadcast([NS, NB // 2, P]),
                            seqm[:, :, None].to_broadcast([NS, NB // 2, P]), ALU.mult).then_inc(g_vz, 1)
            if h >= 1:
                hgrn_store(pool, h - 1)
                if h + 2 < HH:
                    load_states(h + 2)
        hgrn_store(pool, HH - 1)
        pool.wait_ge(g_y, HH)
        pool.wait_ge(stored, 16)
        pool.dma_start(acts[:, C_X1:C_X1 + KC, :].rearrange("p c t -> p (c t)"), xspill).then_inc(x1_loaded, 16)
        def conv_state_out(i):
            pool.wait_ge(e_cso, i + 1)
            pool.dma_start(o["sc_p"][0, 0][:, ds(i * UC, UC)], csn[0:2]).then_inc(stored, 16)
            pool.dma_start(o["sc_s"][0].rearrange("b r d -> (b r) d")[:, ds(i * UC, UC)], csn[32:48]).then_inc(stored, 16)
        loop(pool, 8, conv_state_out)
        for u in range(8):
            pool.wait_ge(f_e, u + 1)
            c = slice(u * UC, u * UC + UC)
            for t in range(2):
                pool.dma_start(o["y_p"][0, t * P:(t + 1) * P, c], ynat[:, t, c]).then_inc(y_out, 16)
            pool.dma_start(o["y_s"].rearrange("b j d -> (b j) d")[:, c], ynat[0:NS, 2, c]).then_inc(y_out, 16)
        pool.wait_ge(y_out, 16 * 24)
        pool.wait_ge(stored, 16 * 17)
        pool.wait_ge(hs_out, 16 * HH)
        pool.wait_ge(hp_out, 16 * HH)
        pool.wait_ge(kv_out, 16 * 18)
        pool.wait_ge(passthru, 32)

    @block.tensor
    def _(pe):
        mm, tr = nc.tensor.matmul, nc.tensor.transpose

        def unit(U, par, oph, opl, opset, between=None):
            b0 = 2 * par
            first = not isinstance(U, int) or U >= 2
            if first:
                if isinstance(U, int):
                    pe.wait_ge(bank_free[par], U // 2)
                else:
                    pe.wait_ge(bank_free[par], U[0])
            base = U if isinstance(U, int) else U[1]
            for q in range(4):
                if q == 2 and between:
                    between()
                pe.wait_ge(lo_ready, 4 * base + q + 1)
                pe.wait_ge(h_ready, KC * opset + QK * q + QK)
                for m in range(2):
                    for k in range(QK):
                        kk = QK * q + k
                        out = pproj[:, b0 + m, 0:T]
                        cs = slice(m * P, m * P + P)
                        mm(out, wh[:, q, k, cs], oph[:, kk, :], start=(kk == 0), stop=False)
                        mm(out, wh[:, q, k, cs], opl[:, kk, :], start=False, stop=False)
                        last = mm(out, wl[:, q, k, cs], oph[:, kk, :], start=False, stop=(kk == KC - 1))
                last.then_inc(quarter_used, 1)

        def ada_accumulate(G, landed, first=False, buf=adaw, sems=s_aq):
            if not first:
                pe.wait_ge(ada_out, G)
            for s in range(4):
                pe.wait_ge(sems[s], landed)
                for j in range(4):
                    last = mm(bank[0][32 * j:32 * j + 32, 0:UC], cond[:, QK * s + j, :], buf[:, s, j, :],
                              start=(s == 0), stop=(s == 3), skip_group_check=True)
                last.then_inc(ada_used, 1)

        def ada_select(G, first=False):
            pe.wait_ge(ada_out, G + 1)
            if not first:
                pe.wait_ge(mod_done, G)
            for m in range(2):
                last = mm(bank[1][:, NSEQ * m:NSEQ * m + NSEQ], adas[:, m * P:m * P + P], sel[:],
                          start=True, stop=True)
            last.then_inc(ada_sel, 1)

        pe.wait_ge(consts, 1)
        pe.wait_ge(s_cin, 32)
        for c in range(KC):
            last = tr(bank[0][:, NSEQ * c:NSEQ * c + NSEQ], cnat[0:NSEQ, 0, c * P:c * P + P], ident[0:NSEQ, 0:NSEQ])
        last.then_inc(s_tp, 1)
        pe.wait_ge(s_vec, 16 * 9)
        tr(bank[1][:, 0:96], vnat1[:, 0, :], ident[0:96, 0:96])
        tr(bank[1][:, 96:96 + 91], vnat2[:, 0, :], ident[0:91, 0:91]).then_inc(s_tp, 1)
        pe.wait_ge(s_scin, 16)
        for c in range(KC):
            last = tr(bank[2][:, 16 * c:16 * c + 16], scnat[:, 0, c * P:c * P + P], ident[0:16, 0:16])
        last.then_inc(s_tp, 1)
        pe.wait_ge(cond_done, 1)
        pe.wait_ge(s_tpe, 3)
        ada_accumulate(0, 16, True)
        ada_select(0, True)
        ada_accumulate(1, 16, buf=adaw2, sems=s_aq2)
        ada_select(1)
        pe.wait_ge(s_xin, 48)
        for c in range(KC):
            if c >= 2:
                pe.wait_ge(xc_act, c - 1)
            for t in range(3):
                r = P if t < 2 else NS
                last = tr(bank[2 + c % 2][:, t * P:t * P + r], xnat[0:r, t, c * P:c * P + P], ident[0:r, 0:r])
            last.then_inc(s_tp, 1)
            if c == KC // 2 - 1:
                ada_accumulate(2, 32)
                ada_select(2)
        ada_accumulate(3, 32, buf=adaw2, sems=s_aq2)
        ada_select(3)

        def norm_sum(layer):
            if layer == 0:
                pe.wait_ge(sqr, KC + 1)
                pe.wait_ge(xc_act, KC)
            else:
                pe.wait_ge(ss_done, KC)
            mm(bank[2][:, 0:T], ones[:], ssq, start=True, stop=True).then_inc(ss_sum, 1)

        pe.wait_ge(consts, 2)
        pe.wait_ge(xc_act, KC)
        mm(bank[3][:, 0:WIN], rep8[:], m8[:, 0, 0:WIN], start=True, stop=True).then_inc(s_tp, 1)
        pe.wait_ge(s_tpe, 4)
        mm(bank[3][:, 0:512], rep8[:], m8[:, 0, WIN:WIN + 512], start=True, stop=True).then_inc(s_tp, 1)
        norm_sum(0)
        with pe.Fori(2, GA // 2) as i:
            ada_accumulate(2 * i, 16 * i + 16)
            ada_select(2 * i)
            ada_accumulate(2 * i + 1, 16 * i + 16, buf=adaw2, sems=s_aq2)
            ada_select(2 * i + 1)

        def head_sums(s):
            pe.wait_ge(n_sq, s + 1)
            if not (isinstance(s, int) and s == 0):
                pe.wait_ge(n_ms, s)
            for m in range(2):
                last = mm(bank[2 + m][:, 0:T], blk[:], soft[:, m * T:m * T + T], start=True, stop=True)
            last.then_inc(n_sum, 1)

        for name, U0, n, w, col, opset, G0 in phases:
            def body(i):
                for p in range(2):
                    if G0 is not None:
                        ada_accumulate(G0 + 2 * i + p, 16 * (G0 + 2 * i + p - GA // 2 + 1))
                    if isinstance(i, int):
                        unit(U0 + 2 * i + p, p, hh, hl, opset)
                    else:
                        unit((i + U0 // 2, i * 2 + U0 + p), p, hh, hl, opset)
                    if G0 is not None:
                        ada_select(G0 + 2 * i + p)
                    if name == "qb":
                        head_sums(2 * i + p + 1)
            loop(pe, n, body)
            if name == "q":
                head_sums(0)

        sc_ps = [bank[2], bank[3], pproj[:, 0, :]]
        pt_ps = [bank[0], pproj[:, 2, :]]
        o_ps = [bank[1], pproj[:, 3, :]]
        pe.wait_ge(bank_free[0], U_OUT0 // 2)
        pe.wait_ge(bank_free[1], U_OUT0 // 2)
        pe.wait_ge(mod_done, 40)
        pe.wait_ge(n_q, 5)
        pe.wait_ge(k_sw, 1)

        def scores(j):
            if j >= 3:
                pe.wait_ge(j_max, j - 2)
            ps = sc_ps[j % 3]
            if j < HEADS:
                kv, rows = j // 4, slice(64 * (j % 2), 64 * (j % 2) + 64)
                q = acts[rows, C_Q + j // 2, :]
                k = acts[rows, C_K + kv // 2, :] if kv % 2 == j % 2 else ksw[rows, kv // 2, :]
                mm(ps[:, 0:128], q[:, 0:128], k[:, 0:128], start=True, stop=True)
                last = mm(ps[:, 128:384], q[:, 128:256], k[:, 0:256], start=True, stop=True)
            else:
                pe.wait_ge(c_sb, j - HEADS + 1)
                pe.wait_ge(q_st, 1)
                for e in range(2):
                    b = 2 * (j - HEADS) + e
                    for kv in range(KVH):
                        kc, rows = kv // 2, slice(64 * (kv % 2), 64 * (kv % 2) + 64)
                        qs = qs2[rows, kc, b, :, :].rearrange("p r j -> p (r j)")
                        out = ps[32 * kv:32 * kv + 32, 192 * e:192 * e + 192]
                        mm(out[:, 0:WIN], qs, kct[rows, b, kc, :], start=True, stop=True)
                        last = mm(out[:, WIN:192], qs, acts[rows, C_K + kc, SEQ:T], start=True, stop=True)
            last.then_inc(j_sc, 1)

        def probs_t(j):
            pe.wait_ge(j_p, j + 1)
            if j >= 2:
                pe.wait_ge(j_ptsb, j - 1)
            pj, ps = p4[:, j % 4, 1:PW - 1], pt_ps[j % 2]
            if j < HEADS:
                for k in range(3):
                    last = tr(ps[:, k * P:k * P + P], pj[:, k * P:k * P + P], ident[:])
            else:
                for e in range(2):
                    tr(ps[:, e * P:e * P + P], pj[:, 192 * e:192 * e + WIN], ident[:])
                    last = tr(ps[0:NS, 256 + e * P:256 + e * P + P], pj[:, 192 * e + WIN:192 * e + 192], ident[:])
            last.then_inc(j_pt, 1)

        def outputs(j):
            pe.wait_ge(j_ptsb, j + 1)
            if j >= 2:
                pe.wait_ge(j_g, j - 1)
            pt, ps = pt2[:, j % 2, :], o_ps[j % 2]
            if j < HEADS:
                kv = j // 4
                rows = slice(64 * (j % 2), 64 * (j % 2) + 64)
                vs = slice(64 * kv, 64 * kv + 64)
                mm(ps[rows, 0:128], vnat[:, 0, vs], pt[:, 0:128], start=True, stop=True)
                mm(ps[rows, 128:256], vnat[:, 0, vs], pt[:, 128:256], start=True, stop=False)
                last = mm(ps[rows, 128:256], vnat[:, 1, vs], pt[:, 256:384], start=False, stop=True)
            else:
                for e in range(2):
                    b = 2 * (j - HEADS) + e
                    for kc in range(2):
                        vs, c = slice(P * kc, P * kc + P), P * e + 64 * kc
                        mm(ps[:, c:c + 64], vc[:, b, vs], pt[:, c:c + 64], start=True, stop=False)
                        last = mm(ps[:, c:c + 64], vnat[0:NS, 2, vs], pt[0:NS, 256 + c:256 + c + 64],
                                  start=False, stop=True)
            last.then_inc(j_o, 1)

        def cached_keys(g):
            if g == 0:
                pe.wait_ge(cache_in, 32)
            else:
                pe.wait_ge(c_sb, g)
            for k in range(4):
                b, kc = 2 * g + k // 2, k % 2
                last = tr(pproj[:, 1, k * P:k * P + P], ckn[:, b, kc * P:kc * P + P], ident[:])
            last.then_inc(c_ps, 1)

        for j in range(3):
            scores(j)
        for t, ps in enumerate((bank[0], bank[1], pproj[:, 3, :])):
            r = P if t < 2 else NS
            for kc in range(2):
                tr(ps[0:r, kc * P:kc * P + P], acts[:, C_K + kc, t * P:t * P + r], ident[:])
                last = tr(ps[0:r, 256 + kc * P:256 + kc * P + P], acts[:, C_V + kc, t * P:t * P + r], ident[:])
            last.then_inc(t_ps, 1)
        pe.wait_ge(t_sb, 3)
        for j in range(20):
            probs_t(j)
            if 4 <= j < 8:
                cached_keys(j - 4)
            if j + 3 < 20:
                scores(j + 3)
            if j >= 1:
                outputs(j - 1)
        outputs(19)

        pe.wait_ge(j_g, 20)
        pe.wait_ge(bank_free[0], U_OUT0 // 2)
        pe.wait_ge(bank_free[1], U_OUT0 // 2)

        def square_sum(h):
            pe.wait_ge(g_osq, h + 1)
            mm(pproj[:, 3, 0:T], ones[:], osq[:], start=True, stop=True).then_inc(g_sum, 1)

        def hgrn_scores(h):
            hbuf = hbufs[h % 2]
            if h >= 1:
                pe.wait_ge(g_ksb, h)
            for t in range(3):
                r = P if t < 2 else NS
                last = tr(bank[3][0:r, t * P:t * P + P], acts[:, C_I + h, t * P:t * P + r], ident[:])
            last.then_inc(g_vt, 1)
            if h >= 1:
                pe.wait_ge(g_st, h)
            pe.wait_ge(g_w, h + 1)
            W = hbuf[:, 0:NL * SEQ].rearrange("p (l t) -> p l t", l=NL)
            WS = hbuf[:, NL * SEQ:NL * SEQ + 3 * NS].rearrange("p (l t) -> p l t", l=3)
            kk, qq = acts[:, C_KB + h, :], acts[:, C_QB + h, :]
            for l in range(NL + 1):
                for c in range(4):
                    out = bank[c // 2][64 * (c % 2):64 * (c % 2) + 64, 64 * l:64 * l + 64]
                    t = slice(64 * c, 64 * c + 64)
                    if l < NL:
                        mm(out, W[:, l, t], W[:, l, t], start=True, stop=True)
                    else:
                        mm(out, kk[:, t], qq[:, t], start=True, stop=True)
            if h >= 1:
                pe.wait_ge(g_onsb, h)
            for l in range(3):
                mm(bank[2][0:64, 64 * l:64 * l + 64], WS[:, l, :], WS[:, l, :], start=True, stop=True)
            mm(bank[2][0:64, 192:256], kk[:, SEQ:T], qq[:, SEQ:T], start=True, stop=True).then_inc(g_sc, 1)
            pe.wait_ge(g_vsb, h + 1)
            ke = hbuf[:, O_KD:O_B]
            for t in range(3):
                r = P if t < 2 else NS
                last = tr(bank[3][0:r, t * P:t * P + P], ke[:, t * P:t * P + r], ident[:])
            last.then_inc(g_kt, 1)

        def prompt_updates(h):
            vn = vns[:, h % 2]
            pe.wait_ge(g_ksb, h + 1)
            if h >= 1:
                pe.wait_ge(g_s, 4 * h)
            for half in range(2):
                rows = slice(64 * half, 64 * half + 64)
                for t in range(2):
                    c = 2 * t + half
                    last = mm(pproj[:, 0, c * P:c * P + P], ken[rows, t, :], vn[rows, t, :], start=True, stop=True)
                last.then_inc(g_u, 1)
                pe.wait_ge(g_u, 3 * h + half + 1)

        def sample_updates(h):
            pe.wait_ge(g_vz, h + 1)
            if h >= 1:
                pe.wait_ge(g_x, h)
            for e in range(2):
                rows = slice(32 * e, 32 * e + 32)
                last = mm(pproj[:, 1 + e, :], ken[rows, 2, :], vz[rows, :, :], start=True, stop=True)
            last.then_inc(g_u, 1)

        def from_sample_states(h):
            pe.wait_ge(g_st, h + 1)
            pe.wait_ge(s0_in[h % 3], 16 * (h // 3) + 16)
            for e in range(2):
                for g in range(4):
                    c = SEQ + 32 * e
                    last = mm(bank[2][32 * g:32 * g + 32, 256 + P * e:256 + P * e + P], qebs[h % 2][:, c:c + 32],
                              s0[:, h % 3, 4 * e + g, :], start=True, stop=True)
            last.then_inc(g_on, 1)

        def head_outputs(h):
            vn, s_t, qeb = vns[:, h % 2], stts[:, h % 2], qebs[h % 2]
            if h >= 1:
                pe.wait_ge(g_ms, h)
            for c in range(4):
                rows, t = slice(64 * (c % 2), 64 * (c % 2) + 64), c // 2
                out = pproj[:, 3, 64 * c:64 * c + 64]
                if c:
                    pe.wait_ge(g_s, 4 * h + c)
                    mm(out, sst[:, c - 1, :], qeb[:, 64 * c:64 * c + 64], start=True, stop=False)
                    pe.wait_ge(g_o, 6 * h + c)
                mm(out, vn[rows, t, :], s_t[rows, t, :], start=(c == 0), stop=True).then_inc(g_o, 1)
            pe.wait_ge(g_o, 6 * h + 4)
            mm(pproj[:, 3, SEQ:T], vn[0:NS, 2, :], s_t[0:NS, 2, :], start=True, stop=False).then_inc(g_o, 1)
            pe.wait_ge(g_onsb, h + 1)
            pe.wait_ge(g_o, 6 * h + 5)
            for e in range(2):
                last = mm(pproj[:, 3, SEQ + 32 * e:SEQ + 32 * e + 32], onat[:, e, :], place[:], start=False, stop=(e == 1))
            last.then_inc(g_o, 1)

        hgrn_scores(0)
        prompt_updates(0)
        sample_updates(0)
        for h in range(HH):
            from_sample_states(h)
            if h + 1 < HH:
                hgrn_scores(h + 1)
            head_outputs(h)
            if h + 1 < HH:
                prompt_updates(h + 1)
            square_sum(h)
            if h + 1 < HH:
                sample_updates(h + 1)
        def spread_roots():
            pe.wait_ge(rsel, 1)
            pe.wait_ge(g_nt, 1)
            for h in range(HH):
                if h >= 2:
                    pe.wait_ge(g_y, h - 1)
                g = slice(32 * (h % 4), 32 * (h % 4) + 32)
                mm(bank[h % 2][:, 0:T], blk[g, :], orow[g, T * (h // 4):T * (h // 4) + T], start=True, stop=True)\
                    .then_inc(g_xb, 1)

        def out0(i):
            for p in range(2):
                first = isinstance(i, int) and p == 0
                unit((i + U_OUT0 // 2, i * 2 + U_OUT0 + p), p, hh, hl, 1, spread_roots if first else None)
        out0(0)
        with pe.Fori(1, 4) as i:
            out0(i)
        norm_sum(1)

        def in1(i):
            ada_accumulate(40 + i, 16 * (41 - GA // 2 + i))
            for k in range(4):
                U = U_IN1 + 4 * i + k
                unit((i * 2 + (U_IN1 + k) // 2, U), k % 2, hh, hl, 2)
            ada_select(40 + i)
            pe.wait_ge(e_cs, 2 * i + 2)
            for m in range(2):
                tr(bank[2][0:2, m * P:m * P + P], cst[:, m, 0:2], ident[:])
                last = tr(bank[3][0:16, m * P:m * P + P], cst[:, m, 2:18], ident[:])
            last.then_inc(e_cst, 1)
        loop(pe, 8, in1)

        def y_rows(u, par):
            pe.wait_ge(f_x, u + 1)
            if not (isinstance(u, int) and u == 0):
                pe.wait_ge(f_e, u)
            for m in range(2):
                for t in range(3):
                    r = P if t < 2 else NS
                    last = tr(bank[t][0:r, m * P:m * P + P], xo[par][:, m, t * P:t * P + r], ident[:])
            last.then_inc(f_t, 1)

        def out1(i):
            first = isinstance(i, int) and i == 0
            for p in range(2):
                unit((i + U_OUT1 // 2, i * 2 + U_OUT1 + p), p, yh, yl, 3)
                if not (first and p == 0):
                    y_rows(2 * i + p - 1, 1 - p)
        out1(0)
        with pe.Fori(1, 3) as i:
            out1(i)
        out1(3)
        y_rows(7, 1)

    @block.scalar
    def _(act):
        A = nc.scalar.activation
        st = Steps(act, act_s)

        def split_hi(U, q):
            act.wait_ge(s_wq[q], 16 * U + 16)
            if not isinstance(U, int) or U > 0:
                act.wait_ge(quarter_used, 4 * U + q - 3)
            A(wh[:, q], raw[:, q], ACT.Copy).then_inc(hi_ready, 1)

        def around(U, evac, last=False):
            if not last:
                for q in range(3):
                    split_hi(U + 1, q)
            if evac:
                act.wait_ge(quarter_used, 4 * U + 4)
                act.wait_ge(hi_ready, 4 * U + 7)
                evac()
            if not last:
                split_hi(U + 1, 3)

        def ada_evac(G, first=False):
            act.wait_ge(ada_used, 4 * G + 4)
            if not first:
                act.wait_ge(ada_sel, G)
            A(adas[:], bank[0][:, 0:UC], ACT.Copy).then_inc(ada_out, 1)

        act.wait_ge(s_tp, 1)
        A(soft[:, 0:KC * NSEQ], bank[0][:, 0:KC * NSEQ], ACT.Sigmoid).then_inc(csig, 1)
        act.wait_ge(s_tp, 2)
        A(vecs[:, 0:187], bank[1][:, 0:187], ACT.Copy).then_inc(vecs_done, 1)
        act.wait_ge(s_tp, 3)
        A(sct[:], bank[2][:, 0:256].rearrange("p (c r) -> p c r", c=KC), ACT.Copy).then_inc(s_tpe, 3)
        ada_evac(0, True)
        ada_evac(1)
        for c in range(KC):
            act.wait_ge(s_tp, 4 + c)
            ps = bank[2 + c % 2][:, 0:T]
            if c >= 2:
                act.wait_ge(sqr, c)
            A(xsq[:, c % 2, :], ps, ACT.Square).then_inc(h_sq, 1)
            A(acts[:, C_X0 + c, :], ps, ACT.Copy).then_inc(xc_act, 1)
            if c == KC // 2 - 1:
                ada_evac(2)
        ada_evac(3)
        act.wait_ge(s_tp, 4 + KC)
        A(smask[:, 0:WIN], bank[3][:, 0:WIN], ACT.Copy).then_inc(s_tpe, 1)
        act.wait_ge(s_tp, 5 + KC)
        A(smask[:, WIN:WIN + 512], bank[3][:, 0:512], ACT.Copy).then_inc(s_tpe, 1)

        def rsqrt(out, in_):
            st(A(out, in_, ACT.Ln))
            st.settle()
            return A(out, out, ACT.Exp, scale=-0.5)

        def token_rsqrt(layer):
            act.wait_ge(ms_ready, layer + 1)
            rsqrt(rstd, hb[:, 0, :]).then_inc(rs_ready, 1)

        def modulate(layer, j, par):
            n = KC // 2 * layer + j + 1
            h = hbs[par]
            act.wait_ge(h_nrm, n)
            for e in range(2):
                sh = mods[:, ds(48 * layer + 2 * j + e, 1), 0:1].rearrange("p c s -> p (c s)")
                s1c = s1[:, ds(2 * j + e, 1), 0:1].rearrange("p c s -> p (c s)")
                last = A(h[:, e, 0:SEQ], h[:, e, 0:SEQ], ACT.Identity, bias=sh, scale=s1c)
            last.then_inc(h_aff, 1)
            act.wait_ge(hb_ready, n)
            act.wait_ge(h_aff, n)
            A(hh[:, ds(2 * j, 2), :], h, ACT.Copy).then_inc(h_hi, 1)

        def head_squares(x, s):
            if not (isinstance(s, int) and s == 0):
                act.wait_ge(n_q, s)
            A(soft[:, 0:2 * T].rearrange("p (m t) -> p m t", m=2), x, ACT.Square).then_inc(n_sq, 1)

        def head_rsqrt(s):
            act.wait_ge(n_ms, s + 1)
            act_y = soft[:, 2 * T:4 * T]
            rsqrt(act_y, soft[:, 0:2 * T]).then_inc(n_y, 1)

        nc.scalar.preload_act_table_set("natural_log_exp_and_others")
        token_rsqrt(0)
        act.wait_ge(lb_exp, 1)
        A(lb[:, 1, :], lb[:, 0, :], ACT.Exp).then_inc(lb_exp, 1)
        with act.Fori(2, GA // 4) as i:
            ada_evac(2 * i)
            ada_evac(2 * i + 1)
        with act.Fori(GA // 4, GA // 2) as i:
            for e in range(2):
                ada_evac(2 * i + e)
                modulate(0, 2 * i + e - GA // 2, e)
        for q in range(4):
            split_hi(0, q)
        for name, U0, n, w, col, opset, G0 in phases:
            def body(i):
                for p in range(2):
                    U = U0 + 2 * i + p
                    if G0 is not None:
                        ada_evac(G0 + 2 * i + p)
                    if name == "qb":
                        head_squares(acts[:, ds(C_Q + 4 * i + 2 * p, 2), :], 2 * i + p + 1)
                    ps = pproj[:, 2 * p:2 * p + 2, 0:T]

                    def store(c, scale=1.0):
                        A(acts[:, ds(c + 4 * i + 2 * p, 2), :], ps, ACT.Copy, scale=scale).then_inc(bank_free[p], 1)

                    def evac():
                        if name == "kv":
                            A(acts[:, C_K + 2 * p:C_K + 2 * p + 2, :], ps, ACT.Copy).then_inc(bank_free[p], 1)
                        elif name == "q":
                            store(C_Q)
                        elif name == "qb":
                            store(C_QB, float(DK) ** -0.5)
                        elif name == "i":
                            store(C_I)
                            n = 2 * i + p
                            act.wait_ge(g_f, n + 1)
                            A(acts[:, ds(C_S + 2 * n, 2), :], acts[:, ds(C_S + 2 * n, 2), :], ACT.Ln, scale=16.0)\
                                .then_inc(g_ln, 1)
                        elif name == "f":
                            A(acts[:, ds(C_S + 4 * i + 2 * p, 2), :], ps, ACT.Sigmoid)
                            A(acts[:, ds(C_KB + 4 * i + 2 * p, 2), :], ps, ACT.Sigmoid, scale=-1.0)\
                                .then_inc(bank_free[p], 1)
                        else:
                            act.wait_ge(bank_free[1 - p], i + U0 // 2 + p)
                            A(hb, ps, ACT.Sigmoid).then_inc(z_sig, 1)
                        if name == "qb":
                            head_rsqrt(2 * i + p + 1)
                    around(U, evac)
            loop(act, n, body, *(((st, 2),) if name == "qb" else ()))
            if name == "kv":
                head_squares(acts[:, C_K:C_K + 2, :], 0)
            if name == "q":
                head_rsqrt(0)

        nc.scalar.preload_act_table_set("natural_log_exp_and_others")
        def decays(h):
            act.wait_ge(g_d, 2 * h + 1)
            hbuf, half = hbufs[h % 2], 4 * SEQ
            A(hbuf[:, 0:half], hbuf[:, 0:half], ACT.Exp).then_inc(g_e, 1)
            A(hbuf[:, O_B:HB], acts[:, C_S + h, :], ACT.Exp)
            act.wait_ge(g_d, 2 * h + 2)
            A(hbuf[:, half:O_B], hbuf[:, half:O_B], ACT.Exp).then_inc(g_e, 1)

        act.wait_ge(k_sw, 1)

        def exps(j):
            act.wait_ge(j_max, j + 1)
            c = 129 if j < HEADS else 193
            pj = p4[:, j % 4, :]
            nm = stmp[:, 8 * (j % 4):8 * (j % 4) + 8]
            A(pj[:, 0:c], pj[:, 0:c], ACT.Exp, bias=nm[:, 0:1], accum_out=nm[:, 2:3])
            A(pj[:, c:PW], pj[:, c:PW], ACT.Exp, bias=nm[:, 1:2], accum_out=nm[:, 3:4]).then_inc(j_exp, 1)

        def scaled(j):
            act.wait_ge(j_rs, j + 1)
            c = 129 if j < HEADS else 193
            pj = p4[:, j % 4, :]
            nm = stmp[:, 8 * (j % 4):8 * (j % 4) + 8]
            A(pj[:, c:PW], pj[:, c:PW], ACT.Copy, scale=nm[:, 5:6]).then_inc(j_p, 1)

        for t, ps in enumerate((bank[0], bank[1], pproj[:, 3, :])):
            r = P if t < 2 else NS
            act.wait_ge(t_ps, t + 1)
            A(knat[0:r, t, :], ps[0:r, 0:256], ACT.Copy)
            A(vnat[0:r, t, :], ps[0:r, 256:512], ACT.Copy).then_inc(t_sb, 1)
        act.wait_ge(s_cst, 48)
        exps(0)
        for j in range(20):
            scaled(j)
            if j + 1 < 20:
                exps(j + 1)
            act.wait_ge(j_pt, j + 1)
            if j >= 2:
                act.wait_ge(j_o, j - 1)
            pt, ps = pt2[:, j % 2, :], (bank[0], pproj[:, 2, :])[j % 2]
            if j < HEADS:
                A(pt[:, 0:384], ps[:, 0:384], ACT.Copy).then_inc(j_ptsb, 1)
            else:
                A(pt[:, 0:256], ps[:, 0:256], ACT.Copy)
                A(pt[0:NS, 256:512], ps[0:NS, 256:512], ACT.Copy).then_inc(j_ptsb, 1)
            if 4 <= j < 8:
                g = j - 4
                act.wait_ge(c_ps, g + 1)
                A(kct[:, 2 * g:2 * g + 2, :, :], pproj[:, 1, :].rearrange("p (b c s) -> p b c s", b=2, c=2), ACT.Copy)\
                    .then_inc(c_sb, 1)

        decays(0)
        act.wait_ge(j_g, 20)
        act.wait_ge(kv_out, 16 * 18)

        def sample_rows(h):
            act.wait_ge(g_on, h + 1)
            A(onat[:], bank[2][:, 256:512].rearrange("p (e v) -> p e v", e=2), ACT.Copy).then_inc(g_onsb, 1)

        def rows_of_v(h):
            act.wait_ge(g_vt, h + 1)
            if h >= 1:
                act.wait_ge(g_vz, h)
            vn = vns[:, h % 2]
            A(vn[:, 0:2, :], bank[3][:, 0:256].rearrange("p (t k) -> p t k", t=2), ACT.Copy)
            A(vn[0:NS, 2, :], bank[3][0:NS, 256:384], ACT.Copy).then_inc(g_vsb, 1)

        def rows_of_k(h):
            act.wait_ge(g_kt, h + 1)
            A(ken[:, 0:2, :], bank[3][:, 0:256].rearrange("p (t k) -> p t k", t=2), ACT.Copy)
            A(ken[0:NS, 2, :], bank[3][0:NS, 256:384], ACT.Copy).then_inc(g_ksb, 1)

        rows_of_v(0)
        rows_of_k(0)
        decays(1)
        for h in range(HH):
            sample_rows(h)
            for n in range(NB):
                end = O_B + SEQ + NJ * n + NJ
                last = A(s0[:, h % 3, n, :], s0[:, h % 3, n, :], ACT.Copy, scale=hbufs[h % 2][:, end - 1:end])
            last.then_inc(g_sd, 1)
            if h + 1 < HH:
                rows_of_v(h + 1)
                rows_of_k(h + 1)
            if h + 2 < HH:
                decays(h + 2)
            if h == HH - 1:
                for c in range(HH):
                    A(hh[:, c, :], acts[:, C_Z + c, :], ACT.Copy).then_inc(h_hi, 1)
            act.wait_ge(g_o, 6 * h + 6)
            if h >= 1:
                act.wait_ge(g_g, h)
            A(osb[:], pproj[:, 3, 0:T], ACT.Copy)
            A(osq[:], pproj[:, 3, 0:T], ACT.Square).then_inc(g_osq, 1)
            act.wait_ge(g_sum, h + 1)
            g = slice(32 * (h % 4), 32 * (h % 4) + 32)
            A(om[g, h // 4, :], pproj[g, 3, 0:T], ACT.Copy).then_inc(g_ms, 1)
        act.wait_ge(g_rt, 1)
        rsqrt(orow, om[:].rearrange("p a t -> p (a t)")).then_inc(g_rt, 1)

        act.wait_ge(g_nt, 1)
        for c in range(HH, KC):
            act.wait_ge(g_y, c - HH + 1)
            A(hh[:, c, :], acts[:, C_Z + c, :], ACT.Copy).then_inc(h_hi, 1)

        def out0(i):
            for p in range(2):
                U = U_OUT0 + 2 * i + p

                def evac():
                    act.wait_ge(xc_new, 2 * i + p + 1)
                    A(hb, acts[:, ds(C_X1 + 4 * i + 2 * p, 2), :], ACT.Square).then_inc(h_sq, 1)
                around(U, evac)
        loop(act, 4, out0)
        token_rsqrt(1)
        for j in range(KC // 2):
            modulate(1, j, j % 2)

        def in1(i):
            ada_evac(40 + i)
            for k in range(4):
                U = U_IN1 + 4 * i + k
                ps = pproj[:, 2 * (k % 2):2 * (k % 2) + 2, 0:T]

                def evac():
                    if k == 0:
                        act.wait_ge(bank_free[1], U_IN1 // 2 + 2 * i - 1)
                        A(u_sb, ps, ACT.Copy).then_inc(bank_free[0], 1)
                    elif k == 3:
                        act.wait_ge(h_ready, 3 * KC + 2 * i)
                        A(sz, ps, ACT.Sigmoid).then_inc(e_z, 1)
                around(U, evac)
                if k == 3:
                    for m in range(2):
                        act.wait_ge(e_y, 2 * i + m + 1)
                        A(yh[:, ds(2 * i + m, 1), :], gc[:, m:m + 1, :], ACT.Copy).then_inc(e_yh, 1)
            act.wait_ge(e_cst, i + 1)
            act.wait_ge(stored, 32 * i + 16)
            A(csn[0:2], bank[2][0:2, 0:UC], ACT.Copy)
            A(csn[32:48], bank[3][0:16, 0:UC], ACT.Copy).then_inc(e_cso, 1)
        loop(act, 8, in1)
        def y_rows(u):
            act.wait_ge(f_t, u + 1)
            for t in range(3):
                r = P if t < 2 else NS
                last = A(ynat[0:r, t, ds(u * UC, UC)], bank[t][0:r, 0:UC], ACT.Copy)
            last.then_inc(f_e, 1)

        def out1(i):
            first, last = (isinstance(i, int) and i == n for n in (0, 3))
            for p in range(2):
                more = not (last and p == 1)
                for q in range(3 if more else 0):
                    split_hi(U_OUT1 + 2 * i + p + 1, q)
                if not (first and p == 0):
                    y_rows(2 * i + p - 1)
                if more:
                    split_hi(U_OUT1 + 2 * i + p + 1, 3)
        out1(0)
        with act.Fori(1, 3) as i:
            out1(i)
        out1(3)
        y_rows(7)

    @block.vector
    def _(dve):
        V = nc.vector
        st = Steps(dve, dve_s)
        tt, tsc, stt = V.tensor_tensor, V.tensor_scalar, V.scalar_tensor_tensor

        def split_lo(U, q):
            dve.wait_ge(hi_ready, 4 * U + q + 1)
            tt(wl[:, q], raw[:, q], wh[:, q].bitcast(F32), ALU.subtract).then_inc(lo_ready, 1)

        def around(U, evac, last=False):
            if not last:
                for q in range(3):
                    split_lo(U + 1, q)
            if evac:
                dve.wait_ge(quarter_used, 4 * U + 4)
                if not last:
                    dve.wait_ge(lo_ready, 4 * U + 7)
                evac()
            if not last:
                split_lo(U + 1, 3)

        def mod_out(G):
            dve.wait_ge(ada_sel, G + 1)
            tt(mods[:, ds(2 * G, 2), :], bank[1][:, 0:2 * NSEQ].rearrange("p (m s) -> p m s", m=2),
               adab[:, ds(2 * G, 2)][:, :, None].to_broadcast([P, 2, NSEQ]), ALU.add).then_inc(mod_done, 1)

        def seqs(ap):
            return ap.rearrange("p (b j) -> p b j", j=NJ)

        dve.wait_ge(csig, 1)
        dve.wait_ge(consts, 1)
        tt(cond[:, :, 0:NSEQ], bank[0][:, 0:KC * NSEQ].rearrange("p (c s) -> p c s", c=KC),
           soft[:, 0:KC * NSEQ].rearrange("p (c s) -> p c s", c=KC), ALU.mult).then_inc(cond_done, 1)
        dve.wait_ge(vecs_done, 1)
        tt(lb[:, 0, :], lbl, lbl, ALU.subtract).then_inc(lb_exp, 1)
        mod_out(0)
        mod_out(1)
        V.memset(ssq, 0.0).then_inc(sqr, 1)
        for c in range(KC):
            dve.wait_ge(h_sq, c + 1)
            dve.wait_ge(sqr, c + 1)
            tt(ssq, ssq, xsq[:, c % 2, :], ALU.add).then_inc(sqr, 1)
            if c == KC // 2 - 1:
                mod_out(2)
        mod_out(3)

        def newton(y, m, t):
            st(tt(t, y, y, ALU.mult))
            st.settle()
            st(stt(t, t, -0.5, m, ALU.mult, ALU.mult))
            st.settle()
            return stt(y, t, 1.5, y, ALU.add, ALU.mult)

        def token_norm(layer):
            dve.wait_ge(ss_sum, layer + 1)
            tsc(hb[:, 0, :], bank[2][:, 0:T], 1.0 / D, EPS, ALU.mult, ALU.add).then_inc(ms_ready, 1)
            dve.wait_ge(rs_ready, layer + 1)
            st(newton(rstd, hb[:, 0, :], hb[:, 1, :]))
            st.settle()

        def scales(layer, j, n):
            return st(stt(s1[:, ds(j, n), :], mods[:, ds(48 * layer + 16 + j, n), :], 1.0,
                          nw[:, ds(16 * layer + j, n)][:, :, None].to_broadcast([P, n, NSEQ]), ALU.add, ALU.mult))

        def modulate(layer, j, par, cx):
            n = KC // 2 * layer + j + 1
            h = hbs[par]
            tt(h, acts[:, ds(cx + 2 * j, 2), :], rstd[:, None, :].to_broadcast([P, 2, T]), ALU.mult).then_inc(h_nrm, 1)
            dve.wait_ge(h_nrm, n)
            hs = h[:, :, SEQ:T].rearrange("p c (b j) -> p c b j", j=NJ)
            s1c = s1[:, ds(2 * j, 2), 1:NSEQ][:, :, :, None].to_broadcast([P, 2, NB, NJ])
            sh = mods[:, ds(48 * layer + 2 * j, 2), 1:NSEQ][:, :, :, None].to_broadcast([P, 2, NB, NJ])
            st(tt(hs, hs, s1c, ALU.mult))
            st.settle()
            tt(hs, hs, sh, ALU.add).then_inc(hb_ready, 1)

        def low_part(layer, j, par):
            dve.wait_ge(h_hi, KC // 2 * layer + KC * layer + j + 1)
            tt(hl[:, ds(2 * j, 2), :], hbs[par], hh[:, ds(2 * j, 2), :].bitcast(F32), ALU.subtract).then_inc(h_ready, 2)

        token_norm(0)
        dve.wait_ge(lb_exp, 2)
        st(V.reciprocal(lb[:, 2, :], lb[:, 1, :]))
        st.settle()
        st(tt(lb[:, 1, :], lb[:, 1, :], lb[:, 2, :], ALU.mult))
        st.settle()
        st(tt(lb[:, 2, :], lb[:, 1, :], lb[:, 1, :], ALU.subtract))
        st.settle()
        st(tsc(lb[:, 3, :], lb[:, 2, :], -1.0, 1.0, ALU.mult, ALU.add))
        st.settle()
        with dve.Fori(2, GA // 4) as i:
            mod_out(2 * i)
            mod_out(2 * i + 1)
        with dve.Fori(GA // 4, GA // 2) as i:
            st.enter(i - GA // 4, 4)
            for e in range(2):
                mod_out(2 * i + e)
                dve.wait_ge(mod_done, 2 * i + e + 1)
                scales(0, 2 * (2 * i + e - GA // 2), 2)
                st.settle()
                modulate(0, 2 * i + e - GA // 2, e, C_X0)
                low_part(0, 2 * i + e - GA // 2, e)
        st.leave(GA // 4)
        for q in range(4):
            split_lo(0, q)

        def head_norm(s, x, w):
            dve.wait_ge(n_sum, s + 1)
            for m in range(2):
                last = tsc(soft[:, m * T:m * T + T], bank[2 + m][:, 0:T], 1.0 / HD, EPS, ALU.mult, ALU.add)
            last.then_inc(n_ms, 1)
            dve.wait_ge(n_y, s + 1)
            y = soft[:, 2 * T:4 * T]
            st(newton(y, soft[:, 0:2 * T], norm[:, 2 * T:4 * T]))
            st.settle()
            stt(x, x, w, y.rearrange("p (m t) -> p m t", m=2), ALU.mult, ALU.mult).then_inc(n_q, 1)

        def forget(n):
            s2, k2 = acts[:, ds(C_S + 2 * n, 2), :], acts[:, ds(C_KB + 2 * n, 2), :]
            for m in range(2):
                lo, om1 = lb[:, 2, ds(2 * n + m, 1)], lb[:, 3, ds(2 * n + m, 1)]
                st(tsc(s2[:, m, :], s2[:, m, :], om1, lo, ALU.mult, ALU.add))
                tsc(k2[:, m, :], k2[:, m, :], om1, None, ALU.mult)
            st.settle()
            tsc(s2, s2, 1e-20, None, ALU.max).then_inc(g_f, 1)
            dve.wait_ge(g_ln, n + 1)
            lnf = soft[:, 0:2 * T].rearrange("p (m t) -> p m t", m=2)
            st(tsc(lnf, s2, LN16, None, ALU.subtract))
            st.settle()
            for m in range(2):
                last = V.tensor_tensor_scan(s2[:, m, :], rmask[:], lnf[:, m, :], 0.0, ALU.mult, ALU.add)
            st(last)
            st.settle()

        dve.wait_ge(s_cst, 48)
        for name, U0, n, w, col, opset, G0 in phases:
            def body(i):
                for p in range(2):
                    U = U0 + 2 * i + p
                    evac = None
                    if name in ("za", "zb"):
                        def evac():
                            dve.wait_ge(z_sig, U - U_ZA + 1)
                            dve.wait_ge(stored, 16)
                            tt(acts[:, ds(C_Z + 2 * (U0 - U_ZA) + 4 * i + 2 * p, 2), :], pproj[:, 2 * p:2 * p + 2, 0:T],
                               hb, ALU.mult).then_inc(bank_free[p], 1)
                    if name == "i":
                        def evac():
                            forget(2 * i + p)
                    if name == "qb":
                        def evac():
                            head_norm(2 * i + p + 1, acts[:, ds(C_Q + 4 * i + 2 * p, 2), :], qn)
                    around(U, evac)
                    if G0 is not None:
                        mod_out(G0 + 2 * i + p)
            loop(dve, n, body, *(((st, {"qb": 6, "i": 8}[name]),) if name in ("qb", "i") else ()))
            if name == "q":
                head_norm(0, acts[:, C_K:C_K + 2, :], kn)

        SPANS = ((0, SEQ, LEVELS), (NL * SEQ, NS, LEVELS[3:]))

        def exponents(h):
            hbuf = hbufs[h % 2]
            b, kd = acts[:, C_S + h, :], hbuf[:, O_KD:O_B]
            for n, (base, width, lv) in enumerate(SPANS):
                bt = b[:, 0:SEQ] if n == 0 else b[:, SEQ:T]
                for l, hf in enumerate(lv):
                    nb = width // (2 * hf)
                    bv = bt.rearrange("p (n e h) -> p n e h", e=2, h=hf)
                    wv = hbuf[:, base + l * width:base + (l + 1) * width].rearrange("p (n e h) -> p n e h", e=2, h=hf)
                    mid = bv[:, :, 0, hf - 1:hf].to_broadcast([P, nb, hf])
                    tt(wv[:, :, 0, :], mid, bv[:, :, 0, :], ALU.subtract)
                    last = tt(wv[:, :, 1, :], bv[:, :, 1, :], mid, ALU.subtract)
                    if n == 0 and l == 3:
                        last.then_inc(g_d, 1)
                c = 64 if n == 0 else NJ
                bv = bt.rearrange("p (n c) -> p n c", c=c)
                kv_ = (kd[:, 0:SEQ] if n == 0 else kd[:, SEQ:T]).rearrange("p (n c) -> p n c", c=c)
                last = tt(kv_, bv[:, :, c - 1:c].to_broadcast([P, width // c, c]), bv, ALU.subtract)
            last.then_inc(g_d, 1)

        def weighted(h):
            dve.wait_ge(g_e, 2 * h + 1)
            hbuf = hbufs[h % 2]
            b, kd = hbuf[:, O_B:HB], hbuf[:, O_KD:O_B]
            kk, qq = acts[:, C_KB + h, :], acts[:, C_QB + h, :]
            for n, (base, width, lv) in enumerate(SPANS):
                t = slice(0, SEQ) if n == 0 else slice(SEQ, T)
                for l, hf in enumerate(lv):
                    if n == 0 and l == 4:
                        dve.wait_ge(g_e, 2 * h + 2)
                    wv = hbuf[:, base + l * width:base + (l + 1) * width].rearrange("p (n e h) -> p n e h", e=2, h=hf)
                    kv_ = kk[:, t].rearrange("p (n e h) -> p n e h", e=2, h=hf)
                    qv = qq[:, t].rearrange("p (n e h) -> p n e h", e=2, h=hf)
                    tt(wv[:, :, 0, :], wv[:, :, 0, :], kv_[:, :, 0, :], ALU.mult)
                    tt(wv[:, :, 1, :], wv[:, :, 1, :], qv[:, :, 1, :], ALU.mult)
            tt(kd, kd, kk, ALU.mult)
            if h >= 2:
                dve.wait_ge(g_o, 6 * h - 6)
            tt(qebs[h % 2][:], b, qq, ALU.mult).then_inc(g_w, 1)

        dve.wait_ge(n_q, 5)
        V.tensor_copy(ksw[0:64], acts[64:128, C_K:C_K + 2, :])
        V.tensor_copy(ksw[64:128], acts[0:64, C_K:C_K + 2, :]).then_inc(k_sw, 1)

        def sample_queries():
            for kv in range(KVH):
                for half in range(2):
                    src, dst = slice(64 * half, 64 * half + 64), slice(64 * (kv % 2), 64 * (kv % 2) + 64)
                    for c in range(2):
                        last = V.tensor_copy(qs2[dst, kv // 2, :, 2 * c + half, :],
                                             seqs(acts[src, C_Q + 2 * kv + c, SEQ:T]))
            last.then_inc(q_st, 1)

        def smax(j):
            dve.wait_ge(j_sc, j + 1)
            if j >= 4:
                dve.wait_ge(j_pt, j - 3)
            pj = p4[:, j % 4, :]
            pv = pj[:, 1:PW - 1]
            ps = (bank[2], bank[3], pproj[:, 0, :])[j % 3]
            nm = stmp[:, 8 * (j % 4):8 * (j % 4) + 8]
            c = 129 if j < HEADS else 193
            sk = sinkp[:, j:j + 1] if j < HEADS else sinks[:, 0:1]
            V.tensor_copy(pj[:, 0:PW:PW - 1], sk.to_broadcast([P, 2]))
            if j < HEADS:
                st(stt(pv, ps[:, 0:384], HD ** -0.5, pmask[:], ALU.mult, ALU.add))
            else:
                b = 2 * (j - HEADS)
                pv, psv = pv.rearrange("p (e k) -> p e k", e=2), ps[:, 0:384].rearrange("p (e k) -> p e k", e=2)
                st(stt(pv[:, :, 0:WIN], psv[:, :, 0:WIN], HD ** -0.5,
                       smask[:, 0:WIN][:, None, :].to_broadcast([P, 2, WIN]), ALU.mult, ALU.add))
                st(stt(pv[:, :, WIN:192], psv[:, :, WIN:192], HD ** -0.5,
                       smask[:, WIN + NS * b:WIN + NS * b + 2 * NS].rearrange("p (e k) -> p e k", e=2), ALU.mult, ALU.add))
            st.settle()
            V.reduce_max(nm[:, 6:7], pj[:, 0:c], AX.X)
            st(V.reduce_max(nm[:, 7:8], pj[:, c:PW], AX.X))
            st.settle()
            tsc(nm[:, 0:2], nm[:, 6:8], -1.0, None, ALU.mult).then_inc(j_max, 1)

        def denominators(j):
            dve.wait_ge(j_exp, j + 1)
            c = 129 if j < HEADS else 193
            pj = p4[:, j % 4, :]
            nm = stmp[:, 8 * (j % 4):8 * (j % 4) + 8]
            st(V.reciprocal(nm[:, 4:6], nm[:, 2:4]))
            st.settle()
            tsc(pj[:, 0:c], pj[:, 0:c], nm[:, 4:5], None, ALU.mult).then_inc(j_rs, 1)

        def gate_a(j):
            dve.wait_ge(j_o, j + 1)
            ps = (bank[1], pproj[:, 3, :])[j % 2]
            if j < HEADS:
                rows = slice(64 * (j % 2), 64 * (j % 2) + 64)
                z = acts[rows, C_Z + j // 2, 0:SEQ]
                tt(z, ps[rows, 0:SEQ], z, ALU.mult).then_inc(j_g, 1)
            else:
                for e in range(2):
                    b = 2 * (j - HEADS) + e
                    v4 = ps[:, P * e:P * e + P].rearrange("p (k v c r j) -> p k v c r j", k=2, v=2, c=2, r=2)
                    z4 = acts[:, C_Z:C_Z + 8, SEQ + NJ * b:SEQ + NJ * b + NJ].rearrange("p (k v c) j -> p k v c j", k=2, v=2)
                    for v in range(2):
                        for r in range(2):
                            z = z4[64 * r:64 * r + 64, :, v]
                            last = tt(z, v4[64 * v:64 * v + 64, :, v, :, r, :], z, ALU.mult)
                last.then_inc(j_g, 1)

        dve.wait_ge(s_cst, 48)
        smax(0)
        smax(1)
        sample_queries()
        for j in range(20):
            denominators(j)
            if j + 2 < 20:
                smax(j + 2)
            if j >= 2:
                gate_a(j - 2)
        exponents(0)
        gate_a(18)
        gate_a(19)
        weighted(0)

        dve.wait_ge(kv_out, 16 * 18)
        def masked(h):
            s_t = stts[:, h % 2]
            dve.wait_ge(g_sc, h + 1)
            for c in range(2):
                st(tt(sctmp[:, c, :], bank[c][:, 0:448], lmask[:].rearrange("p l t -> p (l t)"), ALU.mult))
            st(tt(sctmp[0:NS, 2, 0:256], bank[2][0:NS, 0:256], lmask[0:NS, 3:7, :].rearrange("p l t -> p (l t)"), ALU.mult))
            st.settle()
            for c in range(2):
                V.tensor_reduce(s_t[:, c, :], sctmp[:, c, :].rearrange("p (l t) -> p t l", l=NL + 1), AX.X, ALU.add)
            V.tensor_reduce(s_t[0:NS, 2, :], sctmp[0:NS, 2, 0:256].rearrange("p (l t) -> p t l", l=4), AX.X, ALU.add)\
                .then_inc(g_st, 1)

        def states(h):
            b = hbufs[h % 2][:, O_B:HB]
            dve.wait_ge(g_u, 3 * h + 2)
            if h >= 1:
                dve.wait_ge(hp_out, 16 * h)
            V.tensor_copy(sst[:, 0, :], pproj[:, 0, 0:P]).then_inc(g_s, 1)
            for c in range(1, 4):
                dve.wait_ge(g_s, 4 * h + c)
                stt(sst[:, c, :], sst[:, c - 1, :], b[:, 64 * c + 63:64 * c + 64], pproj[:, 0, c * P:c * P + P],
                    ALU.mult, ALU.add).then_inc(g_s, 1)

        def sample_states(h):
            dve.wait_ge(g_sd, h + 1)
            dve.wait_ge(g_u, 3 * h + 3)
            for e in range(2):
                v = s0[:, h % 3, 4 * e:4 * e + 4, :]
                last = tt(v, v, pproj[:, 1 + e, :].rearrange("p (b v) -> p b v", b=4), ALU.add)
            last.then_inc(g_x, 1)

        def gated(h):
            dve.wait_ge(g_osq, h + 1)
            z = acts[:, C_Z + 8 + h, :]
            tt(z, z, osb[:], ALU.mult).then_inc(g_g, 1)

        def o_low(c):
            dve.wait_ge(h_hi, KC // 2 + c + 1)
            tt(hl[:, c, :], acts[:, C_Z + c, :], hh[:, c, :].bitcast(F32), ALU.subtract).then_inc(h_ready, 1)

        for h in range(HH):
            if h + 1 < HH:
                exponents(h + 1)
            masked(h)
            if h + 1 < HH:
                weighted(h + 1)
            states(h)
            sample_states(h)
            if h >= 1:
                gated(h - 1)
        for c in range(HH):
            o_low(c)
        gated(HH - 1)
        dve.wait_ge(g_ms, HH)
        tsc(om[:], om[:], 1.0 / DK, EPS, ALU.mult, ALU.add).then_inc(g_rt, 1)
        dve.wait_ge(g_rt, 2)
        newton(orow, om[:].rearrange("p a t -> p (a t)"), hbufs[1][:, 2 * T:4 * T]).then_inc(g_nt, 1)

        for h in range(HH):
            z = acts[:, C_Z + HH + h, :]
            dve.wait_ge(g_xb, h + 1)
            stt(z, bank[h % 2][:, 0:T], hn, z, ALU.mult, ALU.mult).then_inc(g_y, 1)
            if h >= 1:
                o_low(HH + h - 1)
        o_low(KC - 1)

        def residual(i, p, gate, out_sem, out):
            for m in range(2):
                c = 4 * i + 2 * p + m
                g = mods[:, ds(gate + c, 1), :].rearrange("p c s -> p (c s)")
                x = acts[:, ds(C_X1 + c, 1), 0:SEQ].rearrange("p c t -> p (c t)")
                y = out[:, m:m + 1, 0:SEQ].rearrange("p c t -> p (c t)")
                ps = pproj[:, 2 * p + m, 0:T]
                st(tt(seqs(gtmp[:, m, :]), seqs(ps[:, SEQ:T]), g[:, 1:NSEQ][:, :, None].to_broadcast([P, NB, NJ]), ALU.mult))
                last = stt(y, ps[:, 0:SEQ], g[:, 0:1], x, ALU.mult, ALU.add)
            last.then_inc(bank_free[p], 1)
            st.settle()
            tt(out[:, :, SEQ:T], acts[:, ds(C_X1 + 4 * i + 2 * p, 2), SEQ:T], gtmp, ALU.add).then_inc(out_sem, 1)

        dve.wait_ge(x1_loaded, 16)
        st(V.memset(ssq, 0.0))

        def out0(i):
            for p in range(2):
                def evac():
                    residual(i, p, 32, xc_new, acts[:, ds(C_X1 + 4 * i + 2 * p, 2), :])
                    dve.wait_ge(h_sq, KC + 2 * i + p + 1)
                    for m in range(2):
                        tt(ssq, ssq, hb[:, m, :], ALU.add).then_inc(ss_done, 1)
                        dve.wait_ge(ss_done, 4 * i + 2 * p + m + 1)
                around(U_OUT0 + 2 * i + p, evac)
        loop(dve, 4, out0, (st, 4))
        scales(1, 0, KC)
        token_norm(1)
        for j in range(KC // 2):
            if j >= 2:
                dve.wait_ge(h_ready, 2 * KC + 2 * j - 2)
            modulate(1, j, j % 2, C_X1)
            if j >= 1:
                low_part(1, j - 1, (j - 1) % 2)
        low_part(1, KC // 2 - 1, 1)

        st(V.memset(cin[:, :, 0:2], 0.0))

        def in1(i):
            for k in range(4):
                U = U_IN1 + 4 * i + k
                ps = pproj[:, 2 * (k % 2):2 * (k % 2) + 2, 0:T]

                def evac():
                    if k == 0:
                        for m in range(2):
                            V.tensor_copy(cin[:, m, 258:338].rearrange("p (b c) -> p b c", c=10)[:, :, 0:2],
                                          sct[:, ds(2 * i + m, 1), :].rearrange("p c (b r) -> p (c b) r", r=2))
                    elif k == 1:
                        dve.wait_ge(bank_free[0], 2 * i + U_IN1 // 2 + 1)
                        tt(cin[:, :, 2:258], ps[:, :, 0:SEQ], u_sb[:, :, 0:SEQ], ALU.mult)
                        for m in range(2):
                            cs = cin[:, m, 258:338].rearrange("p (b c) -> p b c", c=10)
                            last = tt(cs[:, :, 2:10], seqs(ps[:, m, SEQ:T]), seqs(u_sb[:, m, SEQ:T]), ALU.mult)
                        last.then_inc(bank_free[1], 1)
                        dve.wait_ge(bank_free[1], 2 * i + U_IN1 // 2 + 1)
                        for m in range(2):
                            cs = cin[:, m, 258:338].rearrange("p (b c) -> p b c", c=10)
                            cl = cst[:, m, :]
                            V.tensor_copy(cl[:, 0:2], cin[:, m, 256:258])
                            V.tensor_copy(cl[:, 2:18].rearrange("p (b r) -> p b r", r=2), cs[:, :, 8:10]).then_inc(e_cs, 1)
                        for tap in range(3):
                            for m in range(2):
                                w = cw[:, tap, ds(2 * i + m, 1)]
                                x = cin[:, m, tap:tap + 336]
                                if tap == 0:
                                    st(tsc(cv[:, m, :], x, w, None, ALU.mult))
                                else:
                                    st(stt(cv[:, m, :], x, w, cv[:, m, :], ALU.mult, ALU.add))
                            st.settle()
                    elif k == 2:
                        for m in range(2):
                            tt(gc[:, m, 0:SEQ], ps[:, m, 0:SEQ], cv[:, m, 0:SEQ], ALU.mult)
                            cs = cv[:, m, 256:336].rearrange("p (b c) -> p b c", c=10)
                            last = tt(seqs(gc[:, m, SEQ:T]), seqs(ps[:, m, SEQ:T]), cs[:, :, 2:10], ALU.mult)
                        last.then_inc(bank_free[0], 1)
                        dve.wait_ge(bank_free[0], 2 * i + U_IN1 // 2 + 2)
                    else:
                        dve.wait_ge(e_z, i + 1)
                        tt(sz, sz, ps, ALU.mult).then_inc(bank_free[1], 1)
                        dve.wait_ge(bank_free[1], 2 * i + U_IN1 // 2 + 2)
                        for m in range(2):
                            tt(gc[:, m, :], gc[:, m, :], sz[:, m, :], ALU.mult).then_inc(e_y, 1)
                around(U, evac)
                if k == 3:
                    for m in range(2):
                        dve.wait_ge(e_yh, 2 * i + m + 1)
                        tt(yl[:, ds(2 * i + m, 1), :], gc[:, m:m + 1, :], yh[:, ds(2 * i + m, 1), :].bitcast(F32),
                           ALU.subtract).then_inc(h_ready, 1)
            mod_out(40 + i)
        loop(dve, 8, in1, (st, 6))

        def out1(i):
            for p in range(2):
                around(U_OUT1 + 2 * i + p, lambda: residual(i, p, 80, f_x, xo[p]))
        loop(dve, 3, out1, (st, 4))
        around(U_END - 2, lambda: residual(3, 0, 80, f_x, xo[0]))
        around(U_END - 1, lambda: residual(3, 1, 80, f_x, xo[1]), True)

    ctx.close()


_INS = ["x_prompt", "x_sample", "cache_k", "cache_v", "state_hgrn", "state_conv", "c_prompt", "c_sample", "norm_w",
        "ada_w", "ada_b", "even_w_in", "even_w_out", "q_norm_w", "k_norm_w", "attn_sinks", "hgrn_lb_logits",
        "hgrn_norm_w", "odd_w_in", "odd_conv_w", "odd_w_out"]
_OUTS = [("y_p", (1, SEQ, D)), ("y_s", (NB, NJ, D)), ("ck_p", (1, 1, WIN, KVH, HD)), ("cv_p", (1, 1, WIN, KVH, HD)),
         ("sh_p", (1, 1, HH, DK, DK)), ("sc_p", (1, 1, 2, D)), ("ck_s", (1, NB, WIN, KVH, HD)),
         ("cv_s", (1, NB, WIN, KVH, HD)), ("sh_s", (1, NB, HH, DK, DK)), ("sc_s", (1, NB, 2, D))]


def kernel(**inputs):
    import numpy as _np
    import concourse.bacc as _bacc
    from concourse import mybir as _mybir
    from concourse.bass_utils import run_bass_kernel_spmd as _run

    nc = _bacc.Bacc("TRN2", target_bir_lowering=False, num_devices=1)
    arrays, a, o = {}, {}, {}
    for name in _INS:
        arrays[f"in_{name}"] = x = _np.ascontiguousarray(inputs[name])
        a[name] = nc.dram_tensor(f"in_{name}", x.shape, _mybir.dt.from_np(x.dtype), kind="ExternalInput").ap()
    for name, shape in _OUTS:
        o[name] = nc.dram_tensor(f"out_{name}", shape, _mybir.dt.float32, kind="ExternalOutput").ap()
    hybrid_step_kernel(nc, a, o)
    r = _run(nc, [arrays], core_ids=[0])
    return tuple(r.results[0][f"out_{name}"] for name, _ in _OUTS)
```
